# Optimizing a Trainium2 kernel written in Bass

```python
import jax, jax.numpy as jnp
from jax import lax
import numpy as np

D_MODEL = 2048
BATCH = 1
SEQ = 256
DEPTH = 2

MLSTM_WIDTH = D_MODEL
MLSTM_HEADS = 4
MLSTM_HEAD_DIM = MLSTM_WIDTH // MLSTM_HEADS
CHUNK = 128
QK_CONV = 5
FGATE_BIAS_LO = 3.0
FGATE_BIAS_HI = 6.0
CONV_WIDTH = D_MODEL
CONV_KERNEL = 31
EPS = 1e-6

_SIZES = (MLSTM_WIDTH,) * 5 + (4 * MLSTM_HEADS,) + (CONV_WIDTH,) * 3 + (D_MODEL,) * 2
N_IN = int(sum(_SIZES))
_OFFSETS = tuple(int(o) for o in np.cumsum(_SIZES)[:-1])
GATE_OFFSET = 5 * MLSTM_WIDTH

kernel_name = "bidir_mlstm_conformer_conv_gated_hybrid"

def rms_norm(x, w):
    xf = x.astype(jnp.float32)
    y = xf * lax.rsqrt(jnp.mean(xf * xf, axis=-1, keepdims=True) + EPS)
    return (y * w.astype(jnp.float32)).astype(x.dtype)

def layer_norm(x, w, b):
    xf = x.astype(jnp.float32)
    mu = jnp.mean(xf, axis=-1, keepdims=True)
    var = jnp.mean(jnp.square(xf - mu), axis=-1, keepdims=True)
    y = (xf - mu) * lax.rsqrt(var + EPS)
    return (y * w.astype(jnp.float32) + b.astype(jnp.float32)).astype(x.dtype)

def depthwise_conv(x, w):
    K = w.shape[0]
    return lax.conv_general_dilated(
        x, w[:, None, :].astype(x.dtype), window_strides=(1,),
        padding=[(K // 2, K // 2)],
        dimension_numbers=("NWC", "WIO", "NWC"),
        feature_group_count=x.shape[-1])

def mlstm_chunkwise(q, k, v, log_i, log_f):
    N, H, S, dh = q.shape
    nc = S // CHUNK

    def to_chunks(t):
        t = t.reshape((N, H, nc, CHUNK) + t.shape[3:])
        return jnp.moveaxis(t, 2, 0)

    xs = tuple(to_chunks(t) for t in (q, k, v, log_i, log_f))
    causal_in_chunk = jnp.tril(jnp.ones((CHUNK, CHUNK), dtype=bool))

    def step(carry, inp):
        C, n, m = carry
        qj, kj, vj, ij, fj = inp
        g = jnp.cumsum(fj, axis=-1)
        a = g + m[..., None]
        D = g[..., :, None] - g[..., None, :] + ij[..., None, :]
        D = jnp.where(causal_in_chunk, D, -jnp.inf)
        m_row = jnp.maximum(a, jnp.max(D, axis=-1))
        w_intra = jnp.exp(D - m_row[..., None])
        w_inter = jnp.exp(a - m_row)
        s = jnp.einsum("nhld,nhsd->nhls", qj, kj) * w_intra
        num = (jnp.einsum("nhls,nhse->nhle", s, vj)
               + w_inter[..., None] * jnp.einsum("nhld,nhde->nhle", qj, C))
        den = jnp.sum(s, axis=-1) + w_inter * jnp.einsum("nhld,nhd->nhl", qj, n)
        h = num / jnp.maximum(jnp.abs(den), jnp.exp(-m_row))[..., None]
        G = g[..., -1]
        b = G[..., None] - g + ij
        m_new = jnp.maximum(G + m, jnp.max(b, axis=-1))
        wk = jnp.exp(b - m_new[..., None])[..., None] * kj
        decay = jnp.exp(G + m - m_new)
        C_new = decay[..., None, None] * C + jnp.einsum("nhsd,nhse->nhde", wk, vj)
        n_new = decay[..., None] * n + jnp.sum(wk, axis=2)
        return (C_new, n_new, m_new), h

    init = (jnp.zeros((N, H, dh, dh), jnp.float32),
            jnp.zeros((N, H, dh), jnp.float32),
            jnp.zeros((N, H), jnp.float32))
    _, hs = lax.scan(step, init, xs)
    return jnp.moveaxis(hs, 0, 2).reshape(N, H, S, dh)

def hybrid_layer(x, norm_w, w_in, b_in, qk_conv_w, mlstm_norm_w, w_a,
                 dw_w, dw_b, ln_w, ln_b, w_b, w_out):
    B, S, _ = x.shape
    H, dh = MLSTM_HEADS, MLSTM_HEAD_DIM
    f32 = jnp.float32
    hn = rms_norm(x, norm_w)
    u = jnp.einsum("bsd,dn->bsn", hn, w_in) + b_in
    q, k, v, o, z_a, gates, glu_a, glu_b, z_b, g_a, g_b = jnp.split(u, _OFFSETS, axis=-1)

    qk = jax.nn.silu(depthwise_conv(jnp.concatenate([q, k], axis=-1), qk_conv_w))
    q, k = jnp.split(qk, 2, axis=-1)

    def heads(t):
        return t.reshape(B, S, H, dh).transpose(0, 2, 1, 3).astype(f32)

    qh, kh, vh = heads(q), heads(k) * (dh ** -0.5), heads(v)
    gates = gates.astype(f32).reshape(B, S, 4, H).transpose(2, 0, 3, 1)
    i_fw, f_fw, i_bw, f_bw = gates[0], gates[1], gates[2], gates[3]
    flip = lambda t: jnp.flip(t, axis=2)
    both = lambda fw, bw: jnp.concatenate([fw, flip(bw)], axis=0)
    h2 = mlstm_chunkwise(both(qh, qh), both(kh, kh), both(vh, vh),
                         both(i_fw, i_bw), jax.nn.log_sigmoid(both(f_fw, f_bw)))
    ht = h2[:B] + flip(h2[B:])
    ht = jax.nn.sigmoid(heads(o)) * ht
    ht = ht * lax.rsqrt(jnp.mean(ht * ht, axis=-1, keepdims=True) + EPS)
    ya = ht.transpose(0, 2, 1, 3).reshape(B, S, MLSTM_WIDTH) * mlstm_norm_w.astype(f32)
    ya = ya.astype(x.dtype) * jax.nn.silu(z_a)
    y_a = jnp.einsum("bsw,wd->bsd", ya, w_a)

    c = glu_a * jax.nn.sigmoid(glu_b)
    c = depthwise_conv(c, dw_w) + dw_b
    c = jax.nn.silu(layer_norm(c, ln_w, ln_b)) * jax.nn.silu(z_b)
    y_b = jnp.einsum("bsw,wd->bsd", c, w_b)

    merged = jax.nn.sigmoid(g_a) * y_a + jax.nn.sigmoid(g_b) * y_b
    return x + jnp.einsum("bsd,de->bse", merged, w_out)

def setup_inputs(seed: int = 0) -> dict:
    key = jax.random.key(seed)
    ks = jax.random.split(key, 16)
    f32 = jnp.float32
    L, D, H = DEPTH, D_MODEL, MLSTM_HEADS
    nrm = lambda k, shape, scale: scale * jax.random.normal(k, shape, f32)
    x = nrm(ks[0], (BATCH, SEQ, D), 1.0)
    norm_w = 1.0 + nrm(ks[1], (L, D), 0.02)
    w_in = nrm(ks[2], (L, D, N_IN), D ** -0.5)
    b_in = nrm(ks[3], (L, N_IN), 0.02)
    f_bias = jnp.linspace(FGATE_BIAS_LO, FGATE_BIAS_HI, H, dtype=f32)
    b_in = b_in.at[:, GATE_OFFSET + H:GATE_OFFSET + 2 * H].add(f_bias)
    b_in = b_in.at[:, GATE_OFFSET + 3 * H:GATE_OFFSET + 4 * H].add(f_bias)
    qk_conv_w = nrm(ks[4], (L, QK_CONV, 2 * MLSTM_WIDTH), QK_CONV ** -0.5)
    mlstm_norm_w = 1.0 + nrm(ks[5], (L, MLSTM_WIDTH), 0.02)
    w_a = nrm(ks[6], (L, MLSTM_WIDTH, D), MLSTM_WIDTH ** -0.5)
    dw_w = nrm(ks[7], (L, CONV_KERNEL, CONV_WIDTH), CONV_KERNEL ** -0.5)
    dw_b = nrm(ks[8], (L, CONV_WIDTH), 0.02)
    ln_w = 1.0 + nrm(ks[9], (L, CONV_WIDTH), 0.02)
    ln_b = nrm(ks[10], (L, CONV_WIDTH), 0.02)
    w_b = nrm(ks[11], (L, CONV_WIDTH, D), CONV_WIDTH ** -0.5)
    w_out = nrm(ks[12], (L, D, D), D ** -0.5)
    final_norm_w = 1.0 + nrm(ks[13], (D,), 0.02)
    return {"x": x, "norm_w": norm_w, "w_in": w_in, "b_in": b_in,
            "qk_conv_w": qk_conv_w, "mlstm_norm_w": mlstm_norm_w, "w_a": w_a,
            "dw_w": dw_w, "dw_b": dw_b, "ln_w": ln_w, "ln_b": ln_b, "w_b": w_b,
            "w_out": w_out, "final_norm_w": final_norm_w}

def reference(x, norm_w, w_in, b_in, qk_conv_w, mlstm_norm_w, w_a, dw_w, dw_b,
              ln_w, ln_b, w_b, w_out, final_norm_w):
    for l in range(DEPTH):
        x = hybrid_layer(x, norm_w[l], w_in[l], b_in[l], qk_conv_w[l], mlstm_norm_w[l],
                         w_a[l], dw_w[l], dw_b[l], ln_w[l], ln_b[l], w_b[l], w_out[l])
    return rms_norm(x, final_norm_w)


_drawn_inputs = setup_inputs


def setup_inputs(seed=0):
    import zlib

    import numpy as np

    out = dict(_drawn_inputs(seed))
    spreads = {}
    factors = {'norm_w': 3.038,
     'mlstm_norm_w': 6.278,
     'dw_b': 5.337,
     'ln_w': 8.0,
     'ln_b': 8.0,
     'final_norm_w': 2.778}
    for name, (base, spread) in spreads.items():
        noise = np.random.default_rng([zlib.crc32(name.encode()), seed]).standard_normal(out[name].shape)
        drawn = base * np.exp(spread * noise) if base else spread * noise
        out[name] = __import__('jax').numpy.asarray(drawn.astype(out[name].dtype))
    for name, factor in factors.items():
        out[name] = (out[name] * factor).astype(out[name].dtype)
    return out
```

```python
from contextlib import ExitStack

import concourse.bass as bass
from concourse import mybir

F32 = mybir.dt.float32
F32R = mybir.dt.float32r
ALU = mybir.AluOpType
ACT = mybir.ActivationFunctionType
ds = bass.ds

P = 128
L = 2
D = 2048
S = 256
ST = S // P
KT = D // P
H = 4
HT = KT // H
DH = D // H
QK_TAPS = 5
DW_TAPS = 31
PAD = DW_TAPS // 2
CW = S + PAD
EPS = 1e-6
NG = 4 * H
GATE0 = 5 * D
GLU_A, GLU_B, Z_B, G_A, G_B = (GATE0 + NG + i * D for i in range(5))
EXP_CAP = 88.0

QC = 4
KQ = KT // QC
PC = 2 * P
N_GLU, N_HEAD, N_GA, N_ZB, N_GB, N_OUT = KT, 10 * H, KT, KT // 2, KT, KT // 2
AT_GLU = 0
AT_HEAD = AT_GLU + N_GLU
AT_GA = AT_HEAD + N_HEAD
AT_ZB = AT_GA + N_GA
AT_GB = AT_ZB + N_ZB
AT_OUT = AT_GB + N_GB
NP = AT_OUT + N_OUT

B_MAIN, B_CONV = 0, 5 * KT
QK_W = 10 * KT
DW_W = QK_W + QK_TAPS * 2 * KT
NORM_W = DW_W + DW_TAPS * KT
MNORM_W, DW_B, LN_W, LN_B = (NORM_W + i * KT for i in range(1, 5))
PARS = LN_B + KT
PBLK = PARS // P
assert PBLK * P == PARS
Q_T, K_T, V_T, O_T, Z_T = (i * KT for i in range(5))

HEAD_STEPS = 109
LAYER_STEPS = 745


class Steps:

    def __init__(self, eng, sem):
        self.eng, self.sem, self.base, self.k, self.outer = eng, sem, 0, 0, []

    def mark(self, instruction):
        instruction.then_inc(self.sem, 1)
        self.k += 1

    def wait(self, back=0):
        self.eng.wait_ge(self.sem, self.base + (self.k - back))

    def enter(self, index, per):
        self.outer.append((self.base, self.k, per))
        self.base, self.k = self.eng.snap(self.base + index * per + self.k), 0

    def leave(self, rounds):
        base, k, per = self.outer.pop()
        assert self.k == per, (self.k, per)
        self.base, self.k = base, k + rounds * per


def build_trunk(nc, x, norm_w, w_in, b_in, qk_conv_w, mlstm_norm_w, w_a, dw_w, dw_b,
                ln_w, ln_b, w_b, w_out, final_norm_w, out):
    with ExitStack() as ctx:
        def sb(name, shape, dt=F32):
            return ctx.enter_context(nc.sbuf_tensor(name, shape, dt))

        def sem(name):
            return ctx.enter_context(nc.semaphore(name))

        X = sb("X", [P, KT, S])
        Hs = sb("Hs", [P, KT, 2 * S], F32R)
        YC = sb("YC", [P, KT, 2 * S], F32R)
        CP = sb("CP", [P, KT * CW + PAD])
        M = sb("M", [P, KT, S])
        HEAD = sb("HEAD", [P, KT, S])
        QB = sb("QB", [P, HT, S])
        EW = sb("EW", [P, HT, S])
        QPAD = sb("QPAD", [P, 2, S + QK_TAPS - 1])
        T = sb("T", [P, 2, 2, S])
        ROWS = sb("ROWS", [2 * H, 2, S])
        ACC = sb("ACC", [P, 2, S])
        CWT = sb("CWT", [P, 2, DW_TAPS + 1])
        RR = sb("RR", [P, S])
        RAW = sb("RAW", [P, QC, KQ, PC])
        WH = sb("WH", [P, QC, KQ, PC], F32R)
        WL = sb("WL", [P, QC, KQ, PC], F32R)
        PAR = sb("PAR", [P, L * PARS + KT])
        IDENT = sb("IDENT", [P, P])
        ONES = sb("ONES", [P, P])
        GBIAS = sb("GBIAS", [P, L, NG])
        GLOW = sb("GLOW", [P, ST, NG])
        GC = sb("GC", [P, ST, 4, 2 * H])
        CCOL = sb("CCOL", [P, ST, 2 * H])
        EPSC = sb("EPSC", [P, 1])

        K_, V_, VS_, SO_ = (HEAD[:, HT * i:HT * (i + 1), :] for i in range(4))
        KV_ = K_
        GW = HEAD[:, 2 * HT, :].rearrange("p (k g) -> p k g", k=KT)
        GS = YC[:, 0, :].rearrange("p (k g) -> p k g", k=KT)
        F_R, A_R, I_R, G_R, C_R, CB_R, Z_R, N_R = (HEAD[0:2 * H, i, :] for i in range(8))
        RS = EW[0:2 * H, 0:2, :]
        R2 = QPAD[:, :, 2:2 + S]
        XROWS = M[:, :, :].rearrange("p (s a) b -> p s (a b)", s=ST)
        PROWS = CP[:, 0:(L * PBLK + 1) * P].rearrange("p (b c) -> p b c", c=P)

        ps = ctx.enter_context(nc.psum_tensor("ps", [P, 4, 2 * S], F32))
        px = ctx.enter_context(nc.psum_tensor("px", [P, 4, 2 * S], F32))

        rows_in = sem("rows_in")
        raw_in = [sem(f"raw_in{c}") for c in range(QC)]
        gate_in = sem("gate_in")
        hi_made = sem("hi_made")
        lo_made = sem("lo_made")
        multiplied = sem("multiplied")
        low_out = sem("low_out")
        pairs_out = sem("pairs_out")
        ident_made, ones_made, pads_made = sem("ident_made"), sem("ones_made"), sem("pads_made")
        rows_turned = sem("rows_turned")
        par_made = sem("par_made")
        x_turned = sem("x_turned")
        x_in = sem("x_in")
        x_ready = sem("x_ready")
        squared, summed = sem("squared"), sem("summed")
        rms_made = sem("rms_made")
        h_made, h_hi, h_lo = sem("h_made"), sem("h_hi"), sem("h_lo")
        gw_hi, gw_lo = sem("gw_hi"), sem("gw_lo")
        gates_mm, gates_low = sem("gates_mm"), sem("gates_low")
        gcols_made, grows_mm = sem("gcols_made"), sem("grows_mm")
        f_abs, f_exp, f_log = sem("f_abs"), sem("f_exp"), sem("f_log")
        m_made, rows_made, ccol_mm = sem("m_made"), sem("rows_made"), sem("ccol_mm")
        glu_sig = sem("glu_sig")
        qk_summed, qk_silu = sem("qk_summed"), sem("qk_silu")
        rs_made = sem("rs_made")
        scores, m_spread, e_spread = sem("scores"), sem("m_spread"), sem("e_spread")
        e_ready, exp_made, masked = sem("e_ready"), sem("exp_made"), sem("masked")
        heads_seen = sem("heads_seen")
        pw_made = sem("pw_made")
        dens, dens_abs, a_made = sem("dens"), sem("dens_abs"), sem("a_made")
        v_turned, vs_made = sem("v_turned"), sem("vs_made")
        ht_mm, o_sig, ht_made = sem("ht_mm"), sem("o_sig"), sem("ht_made")
        ht_sq, ht_summed, ht_rms = sem("ht_sq"), sem("ht_summed"), sem("ht_rms")
        z_silu, ya_made = sem("z_silu"), sem("ya_made")
        ya_hi, ya_lo = sem("ya_hi"), sem("ya_lo")
        ga_sig, gb_sig = sem("ga_sig"), sem("gb_sig")
        conv_made, mean_mm, centred = sem("conv_made"), sem("mean_mm"), sem("centred")
        c_sq, c_summed, ln_std = sem("c_sq"), sem("c_summed"), sem("ln_std")
        zb_silu, ln_made, ln_silu = sem("zb_silu"), sem("ln_made"), sem("ln_silu")
        cb_made, cb_hi = sem("cb_made"), sem("cb_hi")
        cb_lo = sem("cb_lo")
        m_sum = sem("m_sum")
        m_hi, m_lo = sem("m_hi"), sem("m_lo")
        y_made, y_turned = sem("y_made"), sem("y_turned")
        y_rows = [sem(f"y_rows{s}") for s in range(ST)]
        stored = sem("stored")
        dve_steps, pool_steps = sem("dve_steps"), sem("pool_steps")

        w_in_v = w_in.rearrange("l (k p) n -> l p k n", p=P)
        w_a_v, w_b_v, w_out_v = (w.rearrange("l (k p) n -> l p k n", p=P) for w in (w_a, w_b, w_out))
        out_v = out.rearrange("b (s p) d -> p (b s) d", p=P)

        row_loads = [(XROWS, x.rearrange("b (s p) d -> p (b s) d", p=P)),
                     (GBIAS[:], b_in[:, GATE0:GATE0 + NG].partition_broadcast(P))]

        def param_rows(row, src):
            n, done = src.shape[0], 0
            while done < n:
                at = row + done
                k = min(n - done, P - at % P)
                row_loads.append((PROWS[at % P:at % P + k, at // P, :], src[done:done + k, :]))
                done += k

        for layer in range(L):
            for column, vector in ((B_MAIN, b_in[layer, 0:GATE0]),
                                   (B_CONV, b_in[layer, GATE0 + NG:]),
                                   (NORM_W, norm_w[layer]), (MNORM_W, mlstm_norm_w[layer]),
                                   (DW_B, dw_b[layer]), (LN_W, ln_w[layer]), (LN_B, ln_b[layer])):
                param_rows(layer * PARS + column, vector.rearrange("(t c) -> t c", c=P))
            param_rows(layer * PARS + QK_W, qk_conv_w[layer].rearrange("k (t c) -> (k t) c", c=P))
            param_rows(layer * PARS + DW_W, dw_w[layer].rearrange("k (t c) -> (k t) c", c=P))
        param_rows(L * PARS, final_norm_w.rearrange("(t c) -> t c", c=P))

        def par(l, column, count=1, step=1):
            return PAR[:, ds(l * PARS + column, count, step)]

        def conv_in(tile, tap):
            return CP[:, ds(tile * CW + tap, S)]

        def conv_out(tile, count):
            return CP[:, tile * CW:(tile + count) * CW].rearrange(
                "p (t c) -> p t c", c=CW)[:, :, PAD:CW]

        def spread(rows, count):
            return rows.unsqueeze(1).to_broadcast([P, count, S])

        def buf(g):
            return (EW, QB)[g % 2]

        block = ctx.enter_context(nc.Block())

        @block.sync
        def _(sp):
            for dst, src in row_loads:
                sp.dma_start(dst, src).then_inc(rows_in, 16)

            def load_pair(w, l, col, n):
                for c in range(QC):
                    sp.wait_ge(lo_made, n * QC + (c + 1))
                    sp.dma_start(RAW[:, c, :, :], w[l, :, c * KQ:(c + 1) * KQ, ds(col, PC)]
                                 ).then_inc(raw_in[c], 16)

            with sp.Fori(0, L) as l:
                sp.wait_ge(cb_lo, l * H + 1)
                sp.dma_start(GW, w_in_v[l, :, :, GATE0:GATE0 + NG]).then_inc(gate_in, 16)
                with sp.Fori(0, N_GLU // 2) as j:
                    n = sp.snap(l * NP + AT_GLU + j * 2)
                    load_pair(w_in_v, l, j * PC + GLU_A, n)
                    load_pair(w_in_v, l, j * PC + GLU_B, n + 1)
                with sp.Fori(0, H) as h:
                    n = sp.snap(l * NP + AT_HEAD + h * 10)
                    for i, first in enumerate((K_T, Q_T, V_T, O_T, Z_T)):
                        load_pair(w_in_v, l, h * DH + first * P, n + 2 * i)
                        load_pair(w_in_v, l, h * DH + (first * P + PC), n + (2 * i + 1))
                with sp.Fori(0, N_GA // 2) as j:
                    n = sp.snap(l * NP + AT_GA + j * 2)
                    load_pair(w_in_v, l, j * PC + G_A, n)
                    load_pair(w_a_v, l, j * PC, n + 1)
                with sp.Fori(0, N_ZB) as j:
                    load_pair(w_in_v, l, j * PC + Z_B, sp.snap(l * NP + AT_ZB + j))
                with sp.Fori(0, N_GB // 2) as j:
                    n = sp.snap(l * NP + AT_GB + j * 2)
                    load_pair(w_in_v, l, j * PC + G_B, n)
                    load_pair(w_b_v, l, j * PC, n + 1)
                with sp.Fori(0, N_OUT) as j:
                    load_pair(w_out_v, l, j * PC, sp.snap(l * NP + AT_OUT + j))
            for s in range(ST):
                sp.wait_ge(y_rows[s], 1)
                sp.dma_start(out_v[:, s, :], XROWS[:, s, :]).then_inc(stored, 16)
            sp.wait_ge(stored, 16 * ST)

        @block.gpsimd
        def _(pool):
            steps = Steps(pool, pool_steps)
            steps.mark(nc.gpsimd.memset(IDENT[:], 0.0))
            steps.wait()
            nc.gpsimd.affine_select(out=IDENT[:], in_=IDENT[:], compare_op=ALU.not_equal, fill=1.0,
                                    base=0, pattern=[[-1, P]], channel_multiplier=1
                                    ).then_inc(ident_made, 1)
            steps.mark(nc.gpsimd.memset(GC[:], 0.0))
            steps.mark(nc.gpsimd.memset(QPAD[:], 0.0))
            pool.wait_ge(rows_turned, 1)
            steps.mark(nc.gpsimd.memset(CP[:], 0.0))
            steps.wait()
            pool.sem_inc(pads_made, 1)
            with pool.Fori(0, L) as l:
                with pool.Fori(0, H) as h:
                    u = pool.snap(l * H + h)
                    pool.wait_ge(exp_made, u + 1)
                    pool.sem_inc(heads_seen, 1)
                    for d in range(2):
                        sign = 1 - 2 * d
                        w = EW[:, 2 * d:2 * d + 2, :]
                        nc.gpsimd.affine_select(out=w, in_=w, compare_op=ALU.is_ge, fill=0.0,
                                                base=0, pattern=[[-P * sign, ST], [sign, S]],
                                                channel_multiplier=-sign).then_inc(masked, 1)

        @block.scalar
        def _(act):
            def split_hi(n, c):
                act.wait_ge(raw_in[c], n * 16 + 16)
                act.wait_ge(multiplied, n * QC + (c + 1))
                nc.scalar.copy(WH[:, c, :, :], RAW[:, c, :, :]).then_inc(hi_made, 1)

            def low_half(n, k, bias=None):
                act.wait_ge(multiplied, n * QC + (k + 2) * QC)
                act.wait_ge(pairs_out, n + (k + 1))
                q = k % 2
                if bias is None:
                    nc.scalar.copy(T[:, q, :, :], ps[:, 2 * q:2 * q + 2, S:2 * S]
                                   ).then_inc(low_out, 1)
                    return
                for t in range(2):
                    i = nc.scalar.activation(T[:, q, t, :], ps[:, 2 * q + t, S:2 * S], ACT.Identity,
                                             bias=bias(t))
                i.then_inc(low_out, 1)

            def split_rest(n, k, first=1, last=QC):
                for c in range(first, last):
                    split_hi(n + (k + 1), c)

            def split_and_low(n, k, bias=None):
                split_rest(n, k, 0)
                low_half(n, k, bias)

            act.wait_ge(rows_turned, 1)
            nc.scalar.copy(PAR[:], px[:].rearrange("p a b -> p (a b)")[:, 0:L * PARS + KT]
                           ).then_inc(par_made, 1)
            act.wait_ge(x_turned, 2)
            nc.scalar.copy(X[:, KT // 2:KT, :], px[:].rearrange("p a (b c) -> p (a b) c", c=S)
                           ).then_inc(x_in, 1)

            def square_x(l):
                act.wait_ge(x_ready, l + 1)
                for g in range(4):
                    if g >= 2:
                        act.wait_ge(summed, l * 4 + (g - 1))
                    nc.scalar.activation(buf(g)[:], X[:, 4 * g:4 * g + 4, :], ACT.Square
                                         ).then_inc(squared, 1)
                act.wait_ge(summed, l * 4 + 4)
                nc.scalar.activation(RR[:], px[:, 0, 0:S], ACT.Sqrt, bias=EPSC[:], scale=1.0 / D
                                     ).then_inc(rms_made, 1)

            def sigmoid_out(n, k, where, done):
                act.wait_ge(pairs_out, n + (k + 3))
                nc.scalar.activation(where, where, ACT.Sigmoid).then_inc(done, 1)

            with act.Fori(0, L) as l:
                n0 = act.snap(l * NP)
                act.wait_ge(gate_in, l * 16 + 16)
                nc.scalar.copy(GS[:, :, 0:NG], GW).then_inc(gw_hi, 1)
                square_x(l)
                for c in range(QC):
                    split_hi(n0, c)
                for g in range(4):
                    act.wait_ge(h_made, l * 4 + (g + 1))
                    nc.scalar.copy(Hs[:, 4 * g:4 * g + 4, 0:S], buf(g)[:]).then_inc(h_hi, 1)

                def glu_bias(j, half):
                    return lambda t: par(l, j * 2 + (B_CONV + KT * half + t))

                split_rest(n0, 0, 0)
                act.wait_ge(gates_mm, l + 1)
                nc.scalar.copy(GLOW[:], px[:, 0:ST, NG:2 * NG]).then_inc(gates_low, 1)
                low_half(n0, 0, glu_bias(0, 0))
                split_rest(n0, 1, 0, 1)
                act.wait_ge(grows_mm, l + 1)
                nc.scalar.activation(A_R, px[0:2 * H, 2, S:2 * S], ACT.Abs)
                nc.scalar.copy(I_R, px[0:2 * H, 2, 0:S]).then_inc(f_abs, 1)
                act.wait_ge(f_abs, l + 1)
                nc.scalar.activation(A_R, A_R, ACT.Exp, scale=-1.0).then_inc(f_exp, 1)
                act.wait_ge(f_exp, l + 1)
                nc.scalar.activation(A_R, A_R, ACT.Ln, bias=1.0).then_inc(f_log, 1)
                split_rest(n0, 1)
                low_half(n0, 1, glu_bias(0, 1))
                sigmoid_out(n0, 1, QB[:, 2:4, :], glu_sig)
                split_rest(n0, 2, 0, 1)
                act.wait_ge(m_made, l + 1)
                nc.scalar.activation(ROWS[:, 1, :], N_R, ACT.Exp).then_inc(rows_made, 1)
                split_rest(n0, 2)
                low_half(n0, 2, glu_bias(1, 0))
                split_and_low(n0, 3, glu_bias(1, 1))
                sigmoid_out(n0, 3, QB[:, 2:4, :], glu_sig)
                with act.Fori(2, N_GLU // 2) as j:
                    n = act.snap(l * NP + j * 2)
                    split_and_low(n, 0, glu_bias(j, 0))
                    split_and_low(n, 1, glu_bias(j, 1))
                    sigmoid_out(n, 1, QB[:, 2:4, :], glu_sig)

                with act.Fori(0, H) as h:
                    n = act.snap(l * NP + AT_HEAD + h * 10)
                    u = act.snap(l * H + h)

                    def bias(first):
                        return lambda t: par(l, h * HT + (B_MAIN + first + t))

                    split_and_low(n, 0, bias(K_T))
                    for i, first in enumerate((K_T + 2, Q_T, Q_T + 2, V_T)):
                        split_rest(n, i + 1, 0, 1)
                        act.wait_ge(qk_summed, u * 4 + (i + 1))
                        b = (K_, QB)[i // 2][:, 2 * (i % 2):2 * (i % 2) + 2, :]
                        nc.scalar.activation(b, b, ACT.Silu).then_inc(qk_silu, 1)
                        split_rest(n, i + 1)
                        low_half(n, i + 1, bias(first))
                    split_rest(n, 5, 0, 2)
                    act.wait_ge(e_ready, u + 1)
                    nc.scalar.activation(EW[:], EW[:], ACT.Exp, scale=-1.0).then_inc(exp_made, 1)
                    split_rest(n, 5, 2)
                    low_half(n, 5, bias(V_T + 2))
                    split_rest(n, 6, 0, 1)
                    act.wait_ge(dens, u + 1)
                    nc.scalar.activation(R2, px[:, 1, :].rearrange("p (d s) -> p d s", d=2), ACT.Abs
                                         ).then_inc(dens_abs, 1)
                    split_rest(n, 6)
                    low_half(n, 6, bias(O_T))
                    split_rest(n, 7, 0, 1)
                    act.wait_ge(v_turned, u + 1)
                    nc.scalar.copy(VS_, px[:, 2:4, :].rearrange("p a (b c) -> p (a b) c", c=S)
                                   ).then_inc(vs_made, 1)
                    sigmoid_out(n, 6, SO_[:, 0:2, :], o_sig)
                    split_rest(n, 7)
                    low_half(n, 7, bias(O_T + 2))
                    sigmoid_out(n, 7, SO_[:, 2:4, :], o_sig)
                    split_rest(n, 8, 0, 2)
                    act.wait_ge(ht_made, u + 1)
                    nc.scalar.activation(EW[:], KV_, ACT.Square).then_inc(ht_sq, 1)
                    split_rest(n, 8, 2)
                    low_half(n, 8, bias(Z_T))
                    split_rest(n, 9, 0, 1)
                    act.wait_ge(ht_summed, u + 1)
                    nc.scalar.activation(RR[:], px[:, 0, 0:S], ACT.Sqrt, bias=EPSC[:],
                                         scale=1.0 / DH).then_inc(ht_rms, 1)
                    split_rest(n, 9)
                    low_half(n, 9, bias(Z_T + 2))
                    act.wait_ge(pairs_out, n + 12)
                    nc.scalar.activation(QB[:], QB[:], ACT.Silu).then_inc(z_silu, 1)
                    act.wait_ge(ya_made, u + 1)
                    nc.scalar.copy(YC[:, ds(h * HT, HT), 0:S], KV_).then_inc(ya_hi, 1)

                with act.Fori(0, N_GA // 2) as j:
                    n = act.snap(l * NP + AT_GA + j * 2)
                    split_and_low(n, 0, lambda t: par(l, j * 2 + (B_CONV + 3 * KT + t)))
                    sigmoid_out(n, 0, QB[:, 0:2, :], ga_sig)
                    split_and_low(n, 1)

                n = act.snap(l * NP + AT_ZB)

                def zb_bias(j):
                    return lambda t: par(l, B_CONV + 2 * KT + 2 * j + t)

                def silu_zb(j):
                    act.wait_ge(pairs_out, n + (j + 3))
                    z = HEAD[:, 2 * j:2 * j + 2, :]
                    nc.scalar.activation(z, z, ACT.Silu).then_inc(zb_silu, 1)

                def square_c(g):
                    if g >= 2:
                        act.wait_ge(c_summed, l * 4 + (g - 1))
                    act.wait_ge(centred, l * 4 + (g + 1))
                    nc.scalar.activation(buf(g)[:], conv_out(4 * g, 4), ACT.Square
                                         ).then_inc(c_sq, 1)

                def ln_act(g):
                    act.wait_ge(ln_made, l * 4 + (g + 1))
                    for t in range(4):
                        b = buf(g)[:, t, :]
                        i = nc.scalar.activation(b, b, ACT.Silu, scale=par(l, LN_W + 4 * g + t),
                                                 bias=par(l, LN_B + 4 * g + t))
                    i.then_inc(ln_silu, 1)

                def cb_high(g):
                    act.wait_ge(cb_made, l * 4 + (g + 1))
                    nc.scalar.copy(YC[:, 4 * g:4 * g + 4, 0:S], buf(g)[:]).then_inc(cb_hi, 1)

                split_and_low(n, 0, zb_bias(0))
                split_and_low(n, 1, zb_bias(1))
                split_rest(n, 2, 0)
                square_c(0)
                square_c(1)
                low_half(n, 2, zb_bias(2))
                square_c(2)
                square_c(3)
                split_rest(n, 3, 0, 1)
                act.wait_ge(c_summed, l * 4 + 4)
                nc.scalar.activation(RR[:], px[:, 1, 0:S], ACT.Sqrt, bias=EPSC[:], scale=1.0 / D
                                     ).then_inc(ln_std, 1)
                split_rest(n, 3)
                low_half(n, 3, zb_bias(3))
                for j in range(4):
                    silu_zb(j)
                for g in range(3):
                    split_rest(n, g + 4, 0, 1)
                    ln_act(g)
                    split_rest(n, g + 4, 1, 3)
                    cb_high(g)
                    split_rest(n, g + 4, 3)
                    low_half(n, g + 4, zb_bias(g + 4))
                    silu_zb(g + 4)
                split_rest(n, 7, 0, 1)
                ln_act(3)
                split_rest(n, 7)
                low_half(n, 7, zb_bias(7))
                silu_zb(7)
                cb_high(3)

                def g_b(j, n):
                    split_and_low(n, 0, lambda t: par(l, j * 2 + (B_CONV + 4 * KT + t)))
                    sigmoid_out(n, 0, QB[:, 0:2, :], gb_sig)

                with act.Fori(0, N_GB // 2 - 1) as j:
                    n = act.snap(l * NP + AT_GB + j * 2)
                    g_b(j, n)
                    split_and_low(n, 1)
                n = act.snap(l * NP + (AT_OUT - 2))
                g_b(N_GB // 2 - 1, n)
                split_rest(n, 1, 0)
                act.wait_ge(multiplied, n * QC + 2 * QC)
                for g in range(3):
                    act.wait_ge(m_sum, l * (N_GB // 2) + (2 * g + 3))
                    nc.scalar.copy(Hs[:, 4 * g:4 * g + 4, 0:S], M[:, 4 * g:4 * g + 4, :]
                                   ).then_inc(m_hi, 1)
                low_half(n, 1)
                act.wait_ge(m_sum, l * (N_GB // 2) + (N_GB // 2 + 1))
                nc.scalar.copy(Hs[:, 12:16, 0:S], M[:, 12:16, :]).then_inc(m_hi, 1)

                with act.Fori(0, N_OUT // 2 - 1) as j:
                    n = act.snap(l * NP + AT_OUT + j * 2)
                    split_and_low(n, 0)
                    split_and_low(n, 1)
                n = act.snap(l * NP + (NP - 2))
                split_and_low(n, 0)
                low_half(n, 1)

            square_x(L)
            act.wait_ge(y_turned, 2)
            nc.scalar.copy(XROWS[:, 1, :], px[:].rearrange("p a b -> p (a b)")).then_inc(y_rows[1], 1)

        @block.vector
        def _(dve):
            steps = Steps(dve, dve_steps)
            v = nc.vector

            def split_lo(n, c):
                dve.wait_ge(hi_made, n * QC + (c + 1))
                v.tensor_tensor(WL[:, c, :, :], RAW[:, c, :, :], WH[:, c, :, :].bitcast(F32),
                                ALU.subtract).then_inc(lo_made, 1)

            def pair_out(n, k, dst):
                dve.wait_ge(low_out, n + (k + 1))
                q = k % 2
                v.tensor_tensor(dst, ps[:, 2 * q:2 * q + 2, 0:S], T[:, q, :, :], ALU.add
                                ).then_inc(pairs_out, 1)

            def split_next(n, k):
                for c in range(QC):
                    split_lo(n + (k + 1), c)

            v.memset(EPSC[:], EPS)
            v.memset(ONES[:], 1.0).then_inc(ones_made, 1)
            dve.sem_inc(pairs_out, 2)
            dve.sem_inc(lo_made, QC)
            dve.sem_inc(cb_lo, 1)
            dve.sem_inc(m_sum, 1)
            dve.wait_ge(x_in, 1)
            dve.wait_ge(x_turned, 1)
            v.tensor_copy(X[:, 0:KT // 2, :], ps[:].rearrange("p a (b c) -> p (a b) c", c=S)
                          ).then_inc(x_ready, 1)
            dve.wait_ge(par_made, 1)
            dve.wait_ge(pads_made, 1)

            def inverse_rms(l):
                dve.wait_ge(rms_made, l + 1)
                steps.mark(v.reciprocal(RR[:], RR[:]))
                steps.wait()

            def scale_x(tile, weight, dst):
                return v.scalar_tensor_tensor(out=dst, in0=X[:, tile, :], scalar=weight, in1=RR[:],
                                              op0=ALU.mult, op1=ALU.mult)

            with dve.Fori(0, L) as l:
                steps.enter(l, LAYER_STEPS)
                n0 = dve.snap(l * NP)

                def norm_group(g):
                    for t in range(4):
                        i = scale_x(4 * g + t, par(l, NORM_W + 4 * g + t), buf(g)[:, t, :])
                    i.then_inc(h_made, 1)

                def h_low(g):
                    dve.wait_ge(h_hi, l * 4 + (g + 1))
                    v.tensor_tensor(Hs[:, 4 * g:4 * g + 4, S:2 * S], buf(g)[:],
                                    Hs[:, 4 * g:4 * g + 4, 0:S].bitcast(F32), ALU.subtract
                                    ).then_inc(h_lo, 1)

                dve.wait_ge(gate_in, l * 16 + 16)
                dve.wait_ge(gw_hi, l + 1)
                v.tensor_tensor(GS[:, :, NG:2 * NG], GW, GS[:, :, 0:NG].bitcast(F32), ALU.subtract
                                ).then_inc(gw_lo, 1)
                inverse_rms(l)
                norm_group(0)
                norm_group(1)
                for g in range(2, 4):
                    h_low(g - 2)
                    dve.wait_ge(h_lo, l * 4 + (g - 1))
                    norm_group(g)
                h_low(2)
                h_low(3)
                for c in range(QC):
                    split_lo(n0, c)

                taps = [k for k in range(DW_TAPS) if k != PAD] + [PAD]

                def conv_begin(tile):
                    steps.wait()
                    for t in range(2):
                        steps.mark(v.tensor_copy(CWT[:, t, 0:DW_TAPS],
                                                 par(l, tile + (DW_W + t), DW_TAPS, KT)))
                        steps.mark(v.tensor_copy(CWT[:, t, DW_TAPS:DW_TAPS + 1],
                                                 par(l, tile + (DW_B + t))))

                def conv_taps(tile, first, last):
                    for i in range(first, last):
                        k = taps[i]
                        for t in range(2):
                            steps.wait(1)
                            src, w = conv_in(tile + t, k), CWT[:, t, k:k + 1]
                            if i == 0:
                                steps.mark(v.tensor_scalar(ACC[:, t, :], src, w,
                                                           CWT[:, t, DW_TAPS:DW_TAPS + 1],
                                                           ALU.mult, ALU.add))
                            else:
                                dst = src if k == PAD else ACC[:, t, :]
                                steps.mark(v.scalar_tensor_tensor(
                                    out=dst, in0=src, scalar=w, in1=ACC[:, t, :],
                                    op0=ALU.mult, op1=ALU.add))

                def glu_mul(tile, unit):
                    dve.wait_ge(glu_sig, unit)
                    dst = CP[:, ds(tile * CW, 2 * CW)].rearrange("p (t c) -> p t c", c=CW)
                    steps.mark(v.tensor_tensor(dst[:, :, PAD:CW], QB[:, 0:2, :], QB[:, 2:4, :],
                                               ALU.mult))

                split_lo(n0 + 1, 0)
                dve.wait_ge(gates_low, l + 1)
                steps.mark(v.tensor_tensor(GLOW[:], GLOW[:],
                                           GBIAS[:, ds(l, 1), :].to_broadcast([P, ST, NG]), ALU.add))
                steps.wait()
                for group, (kind, row) in enumerate(((0, 0), (2, 0), (1, H), (3, H))):
                    g = slice(H * group, H * group + H)
                    i = v.tensor_tensor(GC[:, :, kind, row:row + H], px[:, 0:ST, g], GLOW[:, :, g],
                                        ALU.add)
                i.then_inc(gcols_made, 1)
                for c in range(1, QC):
                    split_lo(n0 + 1, c)
                pair_out(n0, 0, QB[:, 0:2, :])
                split_lo(n0 + 2, 0)
                dve.wait_ge(f_abs, l + 1)
                steps.mark(v.tensor_scalar(F_R, px[0:2 * H, 2, S:2 * S], 0.0, None, ALU.min))
                steps.mark(v.memset(Z_R, 0.0))
                steps.wait()
                dve.wait_ge(f_log, l + 1)
                steps.mark(v.tensor_tensor(F_R, F_R, A_R, ALU.subtract))
                steps.wait()
                steps.mark(v.tensor_tensor_scan(G_R, F_R, Z_R, 0.0, ALU.add, ALU.add))
                steps.wait()
                steps.mark(v.tensor_tensor(C_R, I_R, G_R, ALU.subtract))
                steps.wait()
                steps.mark(v.tensor_tensor_scan(ROWS[:, 0, :], C_R, C_R, 0.0, ALU.max, ALU.max))
                steps.mark(v.tensor_copy(CB_R, C_R[:, ::-1]))
                steps.wait(1)
                steps.mark(v.scalar_tensor_tensor(out=N_R, in0=G_R, scalar=-1.0, in1=ROWS[:, 0, :],
                                                  op0=ALU.mult, op1=ALU.subtract))
                steps.wait()
                v.tensor_scalar(N_R, N_R, EXP_CAP, None, ALU.min).then_inc(m_made, 1)
                for c in range(1, QC):
                    split_lo(n0 + 2, c)
                pair_out(n0, 1, QB[:, 2:4, :])
                glu_mul(0, l * (N_GLU // 2) + 1)
                split_next(n0, 2)
                steps.wait()
                pair_out(n0, 2, QB[:, 0:2, :])
                split_lo(n0 + 4, 0)
                dve.wait_ge(ccol_mm, l + 1)
                cc = px[:, 3, 0:4 * ST * H].rearrange("p (s c) -> p s c", s=ST)
                steps.mark(v.tensor_copy(CCOL[:, :, 0:H], cc[:, :, 0:H]))
                steps.mark(v.tensor_copy(CCOL[:, :, H:2 * H], cc[:, :, 3 * H:4 * H]))
                for c in range(1, QC):
                    split_lo(n0 + 4, c)
                pair_out(n0, 3, QB[:, 2:4, :])
                glu_mul(2, l * (N_GLU // 2) + 2)

                with dve.Fori(0, 2) as i:
                    steps.enter(i, 3 + 4 + 2 * DW_TAPS)
                    n = dve.snap(l * NP + 4 + i * 6)
                    duo = dve.snap(i * 2)
                    conv_begin(duo)
                    for j in range(3):
                        for k, dst, first, last in ((2 * j, QB[:, 0:2, :], 10 * j, 10 * j + 5),
                                                    (2 * j + 1, QB[:, 2:4, :], 10 * j + 5,
                                                     10 * j + 10 + j // 2)):
                            split_lo(n + (k + 1), 0)
                            conv_taps(duo, first, first + 2)
                            split_lo(n + (k + 1), 1)
                            conv_taps(duo, first + 2, first + 4)
                            split_lo(n + (k + 1), 2)
                            conv_taps(duo, first + 4, last)
                            split_lo(n + (k + 1), 3)
                            pair_out(n, k, dst)
                        glu_mul(i * 6 + (4 + 2 * j), l * (N_GLU // 2) + i * 3 + (3 + j))
                    steps.leave(2)

                with dve.Fori(0, H) as h:
                    steps.enter(h, HEAD_STEPS)
                    n = dve.snap(l * NP + AT_HEAD + h * 10)
                    u = dve.snap(l * H + h)
                    duo = dve.snap(h * 2 + 4)

                    def with_taps(k, a, b):
                        cut = [a + (b - a) * c // 3 for c in range(4)]
                        for c in range(QC):
                            split_lo(n + (k + 1), c)
                            if c < 3:
                                conv_taps(duo, cut[c], cut[c + 1])

                    def narrow_conv(i, dst, first):
                        dve.wait_ge(pairs_out, n + (i + 3))
                        for tap in range(QK_TAPS):
                            for t in range(2):
                                src = QPAD[:, t, tap:tap + S]
                                w = par(l, h * HT + (QK_W + tap * 2 * KT + first + t))
                                if tap == 0:
                                    steps.mark(v.tensor_scalar(dst[:, t, :], src, w, None, ALU.mult))
                                    continue
                                steps.wait(1)
                                ins = v.scalar_tensor_tensor(out=dst[:, t, :], in0=src, scalar=w,
                                                             in1=dst[:, t, :], op0=ALU.mult,
                                                             op1=ALU.add)
                                if tap == QK_TAPS - 1 and t == 1:
                                    ins.then_inc(qk_summed, 1)
                                else:
                                    steps.mark(ins)

                    def one_head_rows(which):
                        v.tensor_scalar(RS[:, 0, :], ROWS[:, which, :], IDENT[0:2 * H, ds(h, 1)],
                                        None, ALU.mult)
                        v.tensor_scalar(RS[:, 1, :], ROWS[:, which, ::-1],
                                        IDENT[0:2 * H, ds(h + H, 1)], None, ALU.mult
                                        ).then_inc(rs_made, 1)

                    conv_begin(duo)
                    with_taps(0, 0, 4)
                    pair_out(n, 0, QPAD[:, :, 2:2 + S])
                    narrow_conv(0, K_[:, 0:2, :], KT)
                    with_taps(1, 4, 7)
                    dve.wait_ge(qk_summed, u * 4 + 1)
                    pair_out(n, 1, QPAD[:, :, 2:2 + S])
                    narrow_conv(1, K_[:, 2:4, :], KT + 2)
                    with_taps(2, 7, 10)
                    dve.wait_ge(qk_summed, u * 4 + 2)
                    pair_out(n, 2, QPAD[:, :, 2:2 + S])
                    narrow_conv(2, QB[:, 0:2, :], 0)
                    with_taps(3, 10, 13)
                    dve.wait_ge(qk_summed, u * 4 + 3)
                    pair_out(n, 3, QPAD[:, :, 2:2 + S])
                    narrow_conv(3, QB[:, 2:4, :], 2)
                    one_head_rows(0)
                    with_taps(4, 13, 19)
                    pair_out(n, 4, V_[:, 0:2, :])
                    split_lo(n + 6, 0)
                    dve.wait_ge(m_spread, u + 1)
                    for d in range(2):
                        for st in range(ST):
                            i = v.tensor_scalar(EW[:, 2 * d + st, :], px[:, 1, d * S:(d + 1) * S],
                                                CCOL[:, st, ds(h + d * H, 1)], 0.0,
                                                ALU.subtract, ALU.max)
                    i.then_inc(e_ready, 1)
                    split_lo(n + 6, 1)
                    split_lo(n + 6, 2)
                    dve.wait_ge(scores, u + 1)
                    sc = px[:, 0, :].rearrange("p (a b) -> p a b", a=ST)
                    for d in range(2):
                        dve.wait_ge(masked, u * 2 + (d + 1))
                        i = v.scalar_tensor_tensor(out=QB[:, 2 * d:2 * d + 2, :], in0=sc,
                                                   scalar=float(DH) ** -0.5,
                                                   in1=EW[:, 2 * d:2 * d + 2, :],
                                                   op0=ALU.mult, op1=ALU.mult)
                    i.then_inc(pw_made, 1)
                    dve.wait_ge(pw_made, u + 1)
                    dve.wait_ge(rows_made, l + 1)
                    one_head_rows(1)
                    split_lo(n + 6, 3)
                    pair_out(n, 5, V_[:, 2:4, :])
                    split_lo(n + 7, 0)
                    dve.wait_ge(e_spread, u + 1)
                    dve.wait_ge(dens_abs, u + 1)
                    steps.mark(v.tensor_tensor(R2, R2, px[:, 0, :].rearrange("p (a b) -> p a b", a=2),
                                               ALU.max))
                    steps.wait()
                    steps.mark(v.reciprocal(R2[:, 0, :], R2[:, 0, :]))
                    split_lo(n + 7, 1)
                    steps.mark(v.reciprocal(R2[:, 1, :], R2[:, 1, :]))
                    split_lo(n + 7, 2)
                    steps.wait(1)
                    steps.mark(v.tensor_tensor(QB[:, 0:2, :], QB[:, 0:2, :],
                                               spread(R2[:, 0, :], 2), ALU.mult))
                    steps.wait(1)
                    steps.mark(v.tensor_tensor(QB[:, 2:4, :], QB[:, 2:4, :],
                                               spread(R2[:, 1, :], 2), ALU.mult))
                    split_lo(n + 7, 3)
                    steps.wait()
                    v.tensor_tensor(QB[:, 0:2, :], QB[:, 0:2, :], QB[:, 2:4, :], ALU.add
                                    ).then_inc(a_made, 1)
                    pair_out(n, 6, SO_[:, 0:2, :])
                    with_taps(7, 19, 25)
                    pair_out(n, 7, SO_[:, 2:4, :])
                    split_lo(n + 9, 0)
                    dve.wait_ge(ht_mm, u + 1)
                    dve.wait_ge(o_sig, u * 2 + 2)
                    v.tensor_tensor(KV_, px[:, 2:4, :].rearrange("p a (b c) -> p (a b) c", c=S), SO_,
                                    ALU.mult).then_inc(ht_made, 1)
                    split_lo(n + 9, 1)
                    conv_taps(duo, 25, 28)
                    split_lo(n + 9, 2)
                    split_lo(n + 9, 3)
                    pair_out(n, 8, QB[:, 0:2, :])
                    split_lo(n + 10, 0)
                    dve.wait_ge(ht_rms, u + 1)
                    steps.mark(v.reciprocal(RR[:], RR[:]))
                    steps.wait()
                    split_lo(n + 10, 1)
                    conv_taps(duo, 28, DW_TAPS)
                    steps.mark(v.tensor_tensor(KV_, KV_, spread(RR[:], HT), ALU.mult))
                    split_lo(n + 10, 2)
                    split_lo(n + 10, 3)
                    pair_out(n, 9, QB[:, 2:4, :])
                    steps.wait()
                    dve.wait_ge(z_silu, u + 1)
                    for t in range(HT):
                        i = v.scalar_tensor_tensor(out=KV_[:, t, :], in0=KV_[:, t, :],
                                                   scalar=par(l, h * HT + (MNORM_W + t)),
                                                   in1=QB[:, t, :], op0=ALU.mult, op1=ALU.mult)
                    i.then_inc(ya_made, 1)
                    dve.wait_ge(ya_hi, u + 1)
                    v.tensor_tensor(YC[:, ds(h * HT, HT), S:2 * S], KV_,
                                    YC[:, ds(h * HT, HT), 0:S].bitcast(F32), ALU.subtract
                                    ).then_inc(ya_lo, 1)
                    steps.leave(H)

                with dve.Fori(0, 2) as i:
                    steps.enter(i, 4 + 4 + 2 * DW_TAPS)
                    n = dve.snap(l * NP + AT_GA + i * 8)
                    duo = dve.snap(i * 2 + 12)
                    conv_begin(duo)
                    for j in range(4):
                        for k, dst in ((2 * j, QB[:, 0:2, :]), (2 * j + 1, QB[:, 2:4, :])):
                            split_lo(n + (k + 1), 0)
                            split_lo(n + (k + 1), 1)
                            conv_taps(duo, 4 * k, 4 * k + 2)
                            split_lo(n + (k + 1), 2)
                            conv_taps(duo, 4 * k + 2, min(4 * k + 4, DW_TAPS))
                            split_lo(n + (k + 1), 3)
                            pair_out(n, k, dst)
                        dve.wait_ge(pairs_out, n + (2 * j + 4))
                        dve.wait_ge(ga_sig, l * (N_GA // 2) + i * 4 + (j + 1))
                        steps.mark(v.tensor_tensor(M[:, ds(i * 8 + 2 * j, 2), :], QB[:, 0:2, :],
                                                   QB[:, 2:4, :], ALU.mult))
                    steps.leave(2)
                steps.wait()
                dve.sem_inc(conv_made, 1)

                n = dve.snap(l * NP + AT_ZB)

                def scale_c(g):
                    v.tensor_tensor(buf(g)[:], conv_out(4 * g, 4), spread(RR[:], 4), ALU.mult
                                    ).then_inc(ln_made, 1)

                def gate_c(g):
                    dve.wait_ge(ln_silu, l * 4 + (g + 1))
                    dve.wait_ge(zb_silu, l * N_ZB + (2 * g + 2))
                    v.tensor_tensor(buf(g)[:], buf(g)[:], HEAD[:, 4 * g:4 * g + 4, :], ALU.mult
                                    ).then_inc(cb_made, 1)

                def low_c(g):
                    dve.wait_ge(cb_hi, l * 4 + (g + 1))
                    v.tensor_tensor(YC[:, 4 * g:4 * g + 4, S:2 * S], buf(g)[:],
                                    YC[:, 4 * g:4 * g + 4, 0:S].bitcast(F32), ALU.subtract
                                    ).then_inc(cb_lo, 1)

                split_next(n, 0)
                pair_out(n, 0, HEAD[:, 0:2, :])
                split_lo(n + 2, 0)
                dve.wait_ge(mean_mm, l + 1)
                steps.mark(v.tensor_scalar(RR[:], px[:, 0, 0:S], 1.0 / D, None, ALU.mult))
                steps.wait()
                for g in range(4):
                    v.tensor_tensor(conv_out(4 * g, 4), conv_out(4 * g, 4), spread(RR[:], 4),
                                    ALU.subtract).then_inc(centred, 1)
                    if g < 3:
                        split_lo(n + 2, g + 1)
                pair_out(n, 1, HEAD[:, 2:4, :])
                split_next(n, 2)
                pair_out(n, 2, HEAD[:, 4:6, :])
                split_lo(n + 4, 0)
                dve.wait_ge(ln_std, l + 1)
                steps.mark(v.reciprocal(RR[:], RR[:]))
                split_lo(n + 4, 1)
                steps.wait()
                scale_c(0)
                split_lo(n + 4, 2)
                split_lo(n + 4, 3)
                pair_out(n, 3, HEAD[:, 6:8, :])
                for g in range(3):
                    split_lo(n + (g + 5), 0)
                    gate_c(g)
                    split_lo(n + (g + 5), 1)
                    if g > 0:
                        dve.wait_ge(cb_lo, l * 4 + (g + 1))
                    scale_c(g + 1)
                    split_lo(n + (g + 5), 2)
                    dve.wait_ge(cb_made, l * 4 + (g + 1))
                    low_c(g)
                    split_lo(n + (g + 5), 3)
                    pair_out(n, g + 4, HEAD[:, 2 * g + 8:2 * g + 10, :])
                split_next(n, 7)
                pair_out(n, 7, HEAD[:, 14:16, :])
                gate_c(3)
                dve.wait_ge(cb_made, l * 4 + 4)
                low_c(3)

                def add_b(tile, unit, n, k):
                    dve.wait_ge(pairs_out, n + (k + 3))
                    dve.wait_ge(gb_sig, unit)
                    steps.mark(v.tensor_tensor(QB[:, 2:4, :], QB[:, 0:2, :], QB[:, 2:4, :],
                                               ALU.mult))
                    steps.wait()
                    m = M[:, ds(tile, 2), :]
                    v.tensor_tensor(m, m, QB[:, 2:4, :], ALU.add).then_inc(m_sum, 1)

                with dve.Fori(0, N_GB // 2 - 1) as j:
                    steps.enter(j, 1)
                    n = dve.snap(l * NP + AT_GB + j * 2)
                    split_next(n, 0)
                    dve.wait_ge(cb_lo, l * 4 + 5)
                    dve.wait_ge(m_sum, l * (N_GB // 2) + j + 1)
                    pair_out(n, 0, QB[:, 0:2, :])
                    split_next(n, 1)
                    pair_out(n, 1, QB[:, 2:4, :])
                    add_b(j * 2, l * (N_GB // 2) + j + 1, n, 1)
                    steps.leave(N_GB // 2 - 1)
                n = dve.snap(l * NP + AT_OUT)

                def merged_low(g):
                    dve.wait_ge(m_hi, l * 4 + (g + 1))
                    v.tensor_tensor(Hs[:, 4 * g:4 * g + 4, S:2 * S], M[:, 4 * g:4 * g + 4, :],
                                    Hs[:, 4 * g:4 * g + 4, 0:S].bitcast(F32), ALU.subtract
                                    ).then_inc(m_lo, 1)

                split_next(n - 2, 0)
                dve.wait_ge(m_sum, l * (N_GB // 2) + N_GB // 2)
                pair_out(n - 2, 0, QB[:, 0:2, :])
                split_lo(n, 0)
                for g in range(3):
                    merged_low(g)
                    split_lo(n, g + 1)
                pair_out(n - 2, 1, QB[:, 2:4, :])
                add_b(KT - 2, l * (N_GB // 2) + N_GB // 2, n - 2, 1)
                merged_low(3)

                def add_x(tile, n, k):
                    dve.wait_ge(pairs_out, n + (k + 3))
                    xt = X[:, ds(tile, 2), :]
                    return v.tensor_tensor(xt, xt, QB[:, 2 * (k % 2):2 * (k % 2) + 2, :], ALU.add)

                with dve.Fori(0, N_OUT // 2 - 1) as j:
                    steps.enter(j, 2)
                    n = dve.snap(l * NP + AT_OUT + j * 2)
                    for k in range(2):
                        split_next(n, k)
                        if k == 0:
                            dve.wait_ge(m_sum, (l + 1) * (N_GB // 2) + 1)
                            steps.wait()
                        pair_out(n, k, QB[:, 2 * k:2 * k + 2, :])
                        steps.mark(add_x(j * 4 + 2 * k, n, k))
                    steps.leave(N_OUT // 2 - 1)
                n = dve.snap(l * NP + NP - 2)
                split_next(n, 0)
                steps.wait()
                pair_out(n, 0, QB[:, 0:2, :])
                steps.mark(add_x(KT - 4, n, 0))
                pair_out(n, 1, QB[:, 2:4, :])
                add_x(KT - 2, n, 1).then_inc(x_ready, 1)
                steps.leave(L)

            inverse_rms(L)
            for t in range(KT):
                i = scale_x(t, PAR[:, L * PARS + t:L * PARS + t + 1], HEAD[:, t, :])
                if t % 4 == 3:
                    i.then_inc(y_made, 1)
            dve.wait_ge(y_turned, 1)
            v.tensor_copy(XROWS[:, 0, :], ps[:].rearrange("p a b -> p (a b)")).then_inc(y_rows[0], 1)

        @block.tensor
        def _(pe):
            mm = nc.tensor.matmul

            def multiply(n, k, act_in):
                q = k % 2
                for c in range(QC):
                    pe.wait_ge(lo_made, n * QC + (k * QC + QC + c + 1))
                    if c == 0:
                        pe.wait_ge(pairs_out, n + (k + 1))
                    for kk in range(KQ):
                        kt = c * KQ + kk
                        for t in range(2):
                            bank, cols = ps[:, 2 * q + t, :], slice(t * P, t * P + P)
                            mm(bank, WH[:, c, kk, cols], act_in[:, kt, :], start=(kt == 0), stop=False)
                            i = mm(bank[:, S:2 * S], WL[:, c, kk, cols], act_in[:, kt, 0:S],
                                   start=False, stop=(kt == KT - 1))
                    i.then_inc(multiplied, 1)

            pe.sem_inc(multiplied, QC)
            pe.wait_ge(ident_made, 1)
            pe.wait_ge(rows_in, 16 * len(row_loads))
            for b in range(L * PBLK + 1):
                rows = P if b < L * PBLK else KT
                i = nc.tensor.transpose(px[:, b // 4, (b % 4) * P:(b % 4) * P + rows],
                                        PROWS[0:rows, b, :], IDENT[0:rows, 0:rows])
            i.then_inc(rows_turned, 1)
            for half, bank in enumerate((ps, px)):
                if half == 1:
                    pe.wait_ge(par_made, 1)
                for t in range(KT // 2):
                    for s in range(ST):
                        at = (t % 2) * S + s * P
                        tile = half * (KT // 2) + t
                        i = nc.tensor.transpose(bank[:, t // 2, at:at + P],
                                                XROWS[:, s, tile * P:(tile + 1) * P], IDENT[:])
                i.then_inc(x_turned, 1)
            pe.wait_ge(ones_made, 1)
            pe.wait_ge(x_ready, 1)

            def sum_channels(bank, tiles, groups_made, base, done):
                for g in range(4):
                    pe.wait_ge(groups_made, base + (g + 1))
                    for t in range(4):
                        i = mm(px[:, bank, 0:S], ONES[:], tiles(g, t), start=(g == 0 and t == 0),
                               stop=(g == 3 and t == 3))
                    i.then_inc(done, 1)

            def squares(g, t):
                return buf(g)[:, t, :]

            with pe.Fori(0, L) as l:
                n0 = pe.snap(l * NP)
                sum_channels(0, squares, squared, l * 4, summed)
                pe.wait_ge(rms_made, l + 1)

                pe.wait_ge(gw_lo, l + 1)
                for k in range(KT):
                    if k % 4 == 0:
                        pe.wait_ge(h_lo, l * 4 + (k // 4 + 1))
                    for s in range(ST):
                        mm(px[:, s, 0:2 * NG], Hs[:, k, s * P:(s + 1) * P], GS[:, k, 0:2 * NG],
                           start=(k == 0), stop=False)
                        i = mm(px[:, s, NG:2 * NG], Hs[:, k, S + s * P:S + (s + 1) * P],
                               GS[:, k, 0:NG], start=False, stop=(k == KT - 1))
                i.then_inc(gates_mm, 1)

                multiply(n0, 0, Hs)
                pe.wait_ge(gcols_made, l + 1)
                for kind in range(2):
                    for s in range(ST):
                        dst = px[0:2 * H, 2, kind * S + s * P:kind * S + (s + 1) * P]
                        mm(dst, GC[:, s, 2 * kind, :], IDENT[:], start=True, stop=False)
                        i = mm(dst, GC[:, ST - 1 - s, 2 * kind + 1, :], IDENT[:, ::-1],
                               start=False, stop=True)
                i.then_inc(grows_mm, 1)
                multiply(n0, 1, Hs)
                multiply(n0, 2, Hs)
                pe.wait_ge(m_made, l + 1)
                for s in range(ST):
                    for b, rows in enumerate((C_R, CB_R)):
                        at = s * 4 * H + b * 2 * H
                        i = mm(px[:, 3, at:at + 2 * H], rows[:, s * P:(s + 1) * P],
                               IDENT[0:2 * H, 0:2 * H], start=True, stop=True)
                i.then_inc(ccol_mm, 1)
                multiply(n0, 3, Hs)
                with pe.Fori(2, N_GLU // 2) as j:
                    n = pe.snap(l * NP + j * 2)
                    multiply(n, 0, Hs)
                    multiply(n, 1, Hs)

                with pe.Fori(0, H) as h:
                    n = pe.snap(l * NP + AT_HEAD + h * 10)
                    u = pe.snap(l * H + h)

                    def spread_rows(bank):
                        for d in range(2):
                            i = mm(px[:, bank, d * S:(d + 1) * S], ONES[0:2 * H, :], RS[:, d, :],
                                   start=True, stop=True)
                        return i

                    for k in range(5):
                        multiply(n, k, Hs)
                    pe.wait_ge(rs_made, u * 2 + 1)
                    spread_rows(1).then_inc(m_spread, 1)
                    pe.wait_ge(qk_silu, u * 4 + 4)
                    for s in range(ST):
                        for k in range(HT):
                            i = mm(px[:, 0, s * S:(s + 1) * S], K_[:, k, s * P:(s + 1) * P],
                                   QB[:, k, :], start=(k == 0), stop=(k == HT - 1))
                    i.then_inc(scores, 1)
                    multiply(n, 5, Hs)
                    pe.wait_ge(pw_made, u + 1)
                    for d in range(2):
                        for s in range(ST):
                            i = mm(px[:, 1, d * S:(d + 1) * S], ONES[:], QB[:, 2 * d + s, :],
                                   start=(s == 0), stop=(s == ST - 1))
                    i.then_inc(dens, 1)
                    pe.wait_ge(rs_made, u * 2 + 2)
                    spread_rows(0).then_inc(e_spread, 1)
                    multiply(n, 6, Hs)
                    pe.wait_ge(pairs_out, n + 8)
                    for s in range(ST):
                        for k in range(HT):
                            i = nc.tensor.transpose(px[:, 2 + s, k * P:(k + 1) * P],
                                                    V_[:, k, s * P:(s + 1) * P], IDENT[:])
                    i.then_inc(v_turned, 1)
                    multiply(n, 7, Hs)
                    pe.wait_ge(a_made, u + 1)
                    pe.wait_ge(vs_made, u + 1)
                    vs = VS_.rearrange("p (s a) b -> p s (a b)", s=ST)
                    for k in range(HT):
                        for s in range(ST):
                            i = mm(px[:, 2 + k // 2, (k % 2) * S:(k % 2 + 1) * S],
                                   vs[:, s, k * P:(k + 1) * P], QB[:, s, :],
                                   start=(s == 0), stop=(s == ST - 1))
                    i.then_inc(ht_mm, 1)
                    multiply(n, 8, Hs)
                    pe.wait_ge(ht_sq, u + 1)
                    for t in range(HT):
                        i = mm(px[:, 0, 0:S], ONES[:], EW[:, t, :], start=(t == 0), stop=(t == HT - 1))
                    i.then_inc(ht_summed, 1)
                    multiply(n, 9, Hs)

                with pe.Fori(0, N_GA // 2) as j:
                    n = pe.snap(l * NP + AT_GA + j * 2)
                    multiply(n, 0, Hs)
                    pe.wait_ge(ya_lo, l * H + H)
                    multiply(n, 1, YC)

                n = pe.snap(l * NP + AT_ZB)
                multiply(n, 0, Hs)
                pe.wait_ge(conv_made, l + 1)
                for t in range(KT):
                    i = mm(px[:, 0, 0:S], ONES[:], CP[:, t * CW + PAD:(t + 1) * CW],
                           start=(t == 0), stop=(t == KT - 1))
                i.then_inc(mean_mm, 1)
                multiply(n, 1, Hs)
                multiply(n, 2, Hs)
                sum_channels(1, squares, c_sq, l * 4, c_summed)
                multiply(n, 3, Hs)
                with pe.Fori(2, N_ZB // 2) as j:
                    n = pe.snap(l * NP + AT_ZB + j * 2)
                    multiply(n, 0, Hs)
                    multiply(n, 1, Hs)

                with pe.Fori(0, N_GB // 2) as j:
                    n = pe.snap(l * NP + AT_GB + j * 2)
                    multiply(n, 0, Hs)
                    pe.wait_ge(cb_lo, l * 4 + 5)
                    multiply(n, 1, YC)
                with pe.Fori(0, N_OUT // 2) as j:
                    n = pe.snap(l * NP + AT_OUT + j * 2)
                    pe.wait_ge(m_lo, l * 4 + 4)
                    multiply(n, 0, Hs)
                    multiply(n, 1, Hs)

            sum_channels(0, squares, squared, L * 4, summed)
            pe.wait_ge(rms_made, L + 1)
            for s, bank in enumerate((ps, px)):
                for t in range(KT):
                    if s == 0 and t % 4 == 0:
                        pe.wait_ge(y_made, t // 4 + 1)
                    i = nc.tensor.transpose(bank[:, t // 4, (t % 4) * P:(t % 4 + 1) * P],
                                            HEAD[:, t, s * P:(s + 1) * P], IDENT[:])
                i.then_inc(y_turned, 1)


_INS = ["x", "norm_w", "w_in", "b_in", "qk_conv_w", "mlstm_norm_w", "w_a", "dw_w", "dw_b",
        "ln_w", "ln_b", "w_b", "w_out", "final_norm_w"]
_OUT = ((1, S, D), "float32")


def kernel(**inputs):
    import numpy as _np
    import concourse.bacc as _bacc
    from concourse import mybir as _mybir
    from concourse.bass_utils import run_bass_kernel_spmd as _run

    nc = _bacc.Bacc("TRN2", target_bir_lowering=False, num_devices=1)
    arrays, args = {}, []
    for name in _INS:
        a = _np.ascontiguousarray(inputs[name])
        arrays[f"in_{name}_dram"] = a
        args.append(nc.dram_tensor(f"in_{name}_dram", a.shape, _mybir.dt.from_np(a.dtype),
                                   kind="ExternalInput").ap())
    dt = _mybir.dt.from_np(_np.dtype(_OUT[1]))
    args.append(nc.dram_tensor("out_0_dram", _OUT[0], dt, kind="ExternalOutput").ap())
    build_trunk(nc, *args)
    r = _run(nc, [arrays], core_ids=[0])
    return r.results[0]["out_0_dram"]
```

```python
from contextlib import ExitStack

import concourse.bass as bass
from concourse import mybir

F32 = mybir.dt.float32
F32R = mybir.dt.float32r
ALU = mybir.AluOpType
ACT = mybir.ActivationFunctionType
ds = bass.ds

P = 128
L = 2
D = 2048
S = 256
ST = S // P
KT = D // P
H = 4
HT = KT // H
DH = D // H
QK_TAPS = 5
DW_TAPS = 31
PAD = DW_TAPS // 2
CW = S + PAD
EPS = 1e-6
NG = 4 * H
GATE0 = 5 * D
GLU_A, GLU_B, Z_B, G_A, G_B = (GATE0 + NG + i * D for i in range(5))
EXP_CAP = 88.0

QC = 4
KQ = KT // QC
PC = 2 * P
N_GLU, N_HEAD, N_GA, N_ZB, N_GB, N_OUT = KT, 10 * H, KT, KT // 2, KT, KT // 2
AT_GLU = 0
AT_HEAD = AT_GLU + N_GLU
AT_GA = AT_HEAD + N_HEAD
AT_ZB = AT_GA + N_GA
AT_GB = AT_ZB + N_ZB
AT_OUT = AT_GB + N_GB
NP = AT_OUT + N_OUT

B_MAIN, B_CONV = 0, 5 * KT
QK_W = 10 * KT
DW_W = QK_W + QK_TAPS * 2 * KT
NORM_W = DW_W + DW_TAPS * KT
MNORM_W, DW_B, LN_W, LN_B = (NORM_W + i * KT for i in range(1, 5))
PARS = LN_B + KT
PBLK = PARS // P
assert PBLK * P == PARS
Q_T, K_T, V_T, O_T, Z_T = (i * KT for i in range(5))

HEAD_STEPS = 109
LAYER_STEPS = 742


class Steps:

    def __init__(self, eng, sem):
        self.eng, self.sem, self.base, self.k, self.outer = eng, sem, 0, 0, []

    def mark(self, instruction):
        instruction.then_inc(self.sem, 1)
        self.k += 1

    def wait(self, back=0):
        self.eng.wait_ge(self.sem, self.base + (self.k - back))

    def enter(self, index, per):
        self.outer.append((self.base, self.k, per))
        self.base, self.k = self.eng.snap(self.base + index * per + self.k), 0

    def leave(self, rounds):
        base, k, per = self.outer.pop()
        assert self.k == per, (self.k, per)
        self.base, self.k = base, k + rounds * per


def build_trunk(nc, x, norm_w, w_in, b_in, qk_conv_w, mlstm_norm_w, w_a, dw_w, dw_b,
                ln_w, ln_b, w_b, w_out, final_norm_w, out):
    with ExitStack() as ctx:
        def sb(name, shape, dt=F32):
            return ctx.enter_context(nc.sbuf_tensor(name, shape, dt))

        def sem(name):
            return ctx.enter_context(nc.semaphore(name))

        X = sb("X", [P, KT, S])
        Hs = sb("Hs", [P, KT, 2 * S], F32R)
        YC = sb("YC", [P, KT, 2 * S], F32R)
        CP = sb("CP", [P, KT * CW + PAD])
        M = sb("M", [P, KT, S])
        HEAD = sb("HEAD", [P, KT, S])
        QB = sb("QB", [P, HT, S])
        EW = sb("EW", [P, HT, S])
        QPAD = sb("QPAD", [P, 2, S + QK_TAPS - 1])
        T = sb("T", [P, 2, 2, S])
        ROWS = sb("ROWS", [2 * H, 2, S])
        ACC = sb("ACC", [P, 2, S])
        CWT = sb("CWT", [P, 2, DW_TAPS + 1])
        RR = sb("RR", [P, S])
        RAW = sb("RAW", [P, QC, KQ, PC])
        WH = sb("WH", [P, QC, KQ, PC], F32R)
        WL = sb("WL", [P, QC, KQ, PC], F32R)
        PAR = sb("PAR", [P, L * PARS + KT])
        IDENT = sb("IDENT", [P, P])
        ONES = sb("ONES", [P, P])
        GBIAS = sb("GBIAS", [P, L, NG])
        GLOW = sb("GLOW", [P, ST, NG])
        GC = sb("GC", [P, ST, 4, 2 * H])
        CCOL = sb("CCOL", [P, ST, 2 * H])
        EPSC = sb("EPSC", [P, 1])

        K_, V_, VS_, SO_ = (HEAD[:, HT * i:HT * (i + 1), :] for i in range(4))
        KV_ = K_
        GW = HEAD[:, 2 * HT, :].rearrange("p (k g) -> p k g", k=KT)
        GS = YC[:, 0, :].rearrange("p (k g) -> p k g", k=KT)
        F_R, A_R, I_R, G_R, C_R, CB_R, Z_R, N_R = (HEAD[0:2 * H, i, :] for i in range(8))
        RS = EW[0:2 * H, 0:2, :]
        R2 = QPAD[:, :, 2:2 + S]
        XROWS = M[:, :, :].rearrange("p (s a) b -> p s (a b)", s=ST)
        PROWS = CP[:, 0:(L * PBLK + 1) * P].rearrange("p (b c) -> p b c", c=P)

        ps = ctx.enter_context(nc.psum_tensor("ps", [P, 4, 2 * S], F32))
        px = ctx.enter_context(nc.psum_tensor("px", [P, 4, 2 * S], F32))

        x_rows_in = sem("x_rows_in")
        rows_in = sem("rows_in")
        raw_in = [sem(f"raw_in{c}") for c in range(QC)]
        gate_in = sem("gate_in")
        hi_made = sem("hi_made")
        lo_made = sem("lo_made")
        multiplied = sem("multiplied")
        low_out = sem("low_out")
        pairs_out = sem("pairs_out")
        ident_made, ones_made, pads_made = sem("ident_made"), sem("ones_made"), sem("pads_made")
        rows_turned = sem("rows_turned")
        par_made = sem("par_made")
        x_turned = sem("x_turned")
        x_in = sem("x_in")
        squared, sq_added = sem("squared"), sem("sq_added")
        summed = sem("summed")
        rms_made = sem("rms_made")
        h_made, h_hi, h_lo = sem("h_made"), sem("h_hi"), sem("h_lo")
        gw_hi, gw_lo = sem("gw_hi"), sem("gw_lo")
        gates_mm, gates_low = sem("gates_mm"), sem("gates_low")
        gcols_made, grows_mm = sem("gcols_made"), sem("grows_mm")
        f_abs, f_exp, f_log = sem("f_abs"), sem("f_exp"), sem("f_log")
        m_made, rows_made, ccol_mm = sem("m_made"), sem("rows_made"), sem("ccol_mm")
        glu_sig = sem("glu_sig")
        qk_summed, qk_silu = sem("qk_summed"), sem("qk_silu")
        rs_made = sem("rs_made")
        scores, m_spread, e_spread = sem("scores"), sem("m_spread"), sem("e_spread")
        e_ready, exp_made, masked = sem("e_ready"), sem("exp_made"), sem("masked")
        heads_seen = sem("heads_seen")
        pw_made = sem("pw_made")
        dens, dens_abs, a_made = sem("dens"), sem("dens_abs"), sem("a_made")
        v_turned, vs_made = sem("v_turned"), sem("vs_made")
        ht_mm, o_sig, ht_made = sem("ht_mm"), sem("o_sig"), sem("ht_made")
        ht_sq, ht_summed, ht_rms = sem("ht_sq"), sem("ht_summed"), sem("ht_rms")
        z_silu, ya_made = sem("z_silu"), sem("ya_made")
        ya_hi, ya_lo = sem("ya_hi"), sem("ya_lo")
        ga_sig, gb_sig = sem("ga_sig"), sem("gb_sig")
        conv_made, mean_mm, centred = sem("conv_made"), sem("mean_mm"), sem("centred")
        c_sq, c_added = sem("c_sq"), sem("c_added")
        c_summed, ln_std = sem("c_summed"), sem("ln_std")
        zb_silu, ln_made, ln_silu = sem("zb_silu"), sem("ln_made"), sem("ln_silu")
        cb_made, cb_hi = sem("cb_made"), sem("cb_hi")
        cb_lo = sem("cb_lo")
        m_sum = sem("m_sum")
        m_hi, m_lo = sem("m_hi"), sem("m_lo")
        y_made, y_turned, inv_made = sem("y_made"), sem("y_turned"), sem("inv_made")
        y_rows = [sem(f"y_rows{s}") for s in range(ST)]
        stored = sem("stored")
        dve_steps, pool_steps = sem("dve_steps"), sem("pool_steps")

        w_in_v = w_in.rearrange("l (k p) n -> l p k n", p=P)
        w_a_v, w_b_v, w_out_v = (w.rearrange("l (k p) n -> l p k n", p=P) for w in (w_a, w_b, w_out))
        out_v = out.rearrange("b (s p) d -> p (b s) d", p=P)

        row_loads = [(GBIAS[:], b_in[:, GATE0:GATE0 + NG].partition_broadcast(P))]

        def param_rows(row, src):
            n, done = src.shape[0], 0
            while done < n:
                at = row + done
                k = min(n - done, P - at % P)
                row_loads.append((PROWS[at % P:at % P + k, at // P, :], src[done:done + k, :]))
                done += k

        for layer in range(L):
            for column, vector in ((B_MAIN, b_in[layer, 0:GATE0]),
                                   (B_CONV, b_in[layer, GATE0 + NG:]),
                                   (NORM_W, norm_w[layer]), (MNORM_W, mlstm_norm_w[layer]),
                                   (DW_B, dw_b[layer]), (LN_W, ln_w[layer]), (LN_B, ln_b[layer])):
                param_rows(layer * PARS + column, vector.rearrange("(t c) -> t c", c=P))
            param_rows(layer * PARS + QK_W, qk_conv_w[layer].rearrange("k (t c) -> (k t) c", c=P))
            param_rows(layer * PARS + DW_W, dw_w[layer].rearrange("k (t c) -> (k t) c", c=P))
        param_rows(L * PARS, final_norm_w.rearrange("(t c) -> t c", c=P))

        def par(l, column, count=1, step=1):
            return PAR[:, ds(l * PARS + column, count, step)]

        def conv_in(tile, tap):
            return CP[:, ds(tile * CW + tap, S)]

        def conv_out(tile, count):
            return CP[:, tile * CW:(tile + count) * CW].rearrange(
                "p (t c) -> p t c", c=CW)[:, :, PAD:CW]

        def spread(rows, count):
            return rows.unsqueeze(1).to_broadcast([P, count, S])

        def buf(g):
            return (EW, QB)[g % 2]

        block = ctx.enter_context(nc.Block())

        @block.sync
        def _(sp):
            sp.dma_start(XROWS, x.rearrange("b (s p) d -> p (b s) d", p=P)).then_inc(x_rows_in, 16)
            for dst, src in row_loads:
                sp.dma_start(dst, src).then_inc(rows_in, 16)

            def load_pair(w, l, col, n):
                for c in range(QC):
                    sp.wait_ge(lo_made, n * QC + (c + 1))
                    sp.dma_start(RAW[:, c, :, :], w[l, :, c * KQ:(c + 1) * KQ, ds(col, PC)]
                                 ).then_inc(raw_in[c], 16)

            with sp.Fori(0, L) as l:
                load_pair(w_in_v, l, GLU_A, sp.snap(l * NP))
                sp.wait_ge(cb_lo, l * H + 1)
                sp.dma_start(GW, w_in_v[l, :, :, GATE0:GATE0 + NG]).then_inc(gate_in, 16)
                load_pair(w_in_v, l, GLU_B, sp.snap(l * NP + 1))
                with sp.Fori(1, N_GLU // 2) as j:
                    n = sp.snap(l * NP + AT_GLU + j * 2)
                    load_pair(w_in_v, l, j * PC + GLU_A, n)
                    load_pair(w_in_v, l, j * PC + GLU_B, n + 1)
                with sp.Fori(0, H) as h:
                    n = sp.snap(l * NP + AT_HEAD + h * 10)
                    for i, first in enumerate((K_T, Q_T, V_T, O_T, Z_T)):
                        load_pair(w_in_v, l, h * DH + first * P, n + 2 * i)
                        load_pair(w_in_v, l, h * DH + (first * P + PC), n + (2 * i + 1))
                with sp.Fori(0, N_GA // 2) as j:
                    n = sp.snap(l * NP + AT_GA + j * 2)
                    load_pair(w_in_v, l, j * PC + G_A, n)
                    load_pair(w_a_v, l, j * PC, n + 1)
                with sp.Fori(0, N_ZB) as j:
                    load_pair(w_in_v, l, j * PC + Z_B, sp.snap(l * NP + AT_ZB + j))
                with sp.Fori(0, N_GB // 2) as j:
                    n = sp.snap(l * NP + AT_GB + j * 2)
                    load_pair(w_in_v, l, j * PC + G_B, n)
                    load_pair(w_b_v, l, j * PC, n + 1)
                with sp.Fori(0, N_OUT) as j:
                    load_pair(w_out_v, l, j * PC, sp.snap(l * NP + AT_OUT + j))
            for s in range(ST):
                sp.wait_ge(y_rows[s], 1)
                sp.dma_start(out_v[:, s, :], XROWS[:, s, :]).then_inc(stored, 16)
            sp.wait_ge(stored, 16 * ST)

        @block.gpsimd
        def _(pool):
            steps = Steps(pool, pool_steps)
            steps.mark(nc.gpsimd.memset(IDENT[:], 0.0))
            steps.wait()
            nc.gpsimd.affine_select(out=IDENT[:], in_=IDENT[:], compare_op=ALU.not_equal, fill=1.0,
                                    base=0, pattern=[[-1, P]], channel_multiplier=1
                                    ).then_inc(ident_made, 1)
            steps.mark(nc.gpsimd.memset(GC[:], 0.0))
            steps.mark(nc.gpsimd.memset(QPAD[:], 0.0))
            pool.wait_ge(rows_turned, 1)
            steps.mark(nc.gpsimd.memset(CP[:], 0.0))
            steps.wait()
            pool.sem_inc(pads_made, 1)
            with pool.Fori(0, L) as l:
                with pool.Fori(0, H) as h:
                    u = pool.snap(l * H + h)
                    pool.wait_ge(exp_made, u + 1)
                    pool.sem_inc(heads_seen, 1)
                    for d in range(2):
                        sign = 1 - 2 * d
                        w = EW[:, 2 * d:2 * d + 2, :]
                        nc.gpsimd.affine_select(out=w, in_=w, compare_op=ALU.is_ge, fill=0.0,
                                                base=0, pattern=[[-P * sign, ST], [sign, S]],
                                                channel_multiplier=-sign).then_inc(masked, 1)

        @block.scalar
        def _(act):
            def split_hi(n, c):
                act.wait_ge(raw_in[c], n * 16 + 16)
                act.wait_ge(multiplied, n * QC + (c + 1))
                nc.scalar.copy(WH[:, c, :, :], RAW[:, c, :, :]).then_inc(hi_made, 1)

            def low_half(n, k, bias=None):
                act.wait_ge(multiplied, n * QC + (k + 2) * QC)
                act.wait_ge(pairs_out, n + (k + 1))
                q = k % 2
                if bias is None:
                    nc.scalar.copy(T[:, q, :, :], ps[:, 2 * q:2 * q + 2, S:2 * S]
                                   ).then_inc(low_out, 1)
                    return
                for t in range(2):
                    i = nc.scalar.activation(T[:, q, t, :], ps[:, 2 * q + t, S:2 * S], ACT.Identity,
                                             bias=bias(t))
                i.then_inc(low_out, 1)

            def split_rest(n, k, first=1, last=QC):
                for c in range(first, last):
                    split_hi(n + (k + 1), c)

            def split_and_low(n, k, bias=None):
                split_rest(n, k, 0)
                low_half(n, k, bias)

            def square_duo(unit, tile, q):
                act.wait_ge(sq_added, unit - 1)
                nc.scalar.activation(EW[:, 2 * q:2 * q + 2, :], X[:, ds(tile, 2), :], ACT.Square
                                     ).then_inc(squared, 1)

            act.wait_ge(x_turned, 2)
            nc.scalar.copy(X[:, KT // 2:KT, :], px[:].rearrange("p a (b c) -> p (a b) c", c=S)
                           ).then_inc(x_in, 1)
            act.wait_ge(x_in, 1)
            act.wait_ge(pairs_out, 2)
            for d in range(KT // 2 - 1):
                if d < 2:
                    nc.scalar.activation(EW[:, 2 * d:2 * d + 2, :], X[:, 2 * d:2 * d + 2, :],
                                         ACT.Square).then_inc(squared, 1)
                else:
                    square_duo(d, 2 * d, d % 2)
            act.wait_ge(rows_turned, 1)
            nc.scalar.copy(PAR[:], px[:].rearrange("p a b -> p (a b)")[:, 0:L * PARS + KT]
                           ).then_inc(par_made, 1)

            def sigmoid_out(n, k, where, done):
                act.wait_ge(pairs_out, n + (k + 3))
                nc.scalar.activation(where, where, ACT.Sigmoid).then_inc(done, 1)

            with act.Fori(0, L) as l:
                n0 = act.snap(l * NP)
                split_hi(n0, 0)
                act.wait_ge(pairs_out, n0 + 2)
                square_duo(l * (KT // 2) + (KT // 2 - 1), KT - 2, 1)
                split_hi(n0, 1)
                act.wait_ge(summed, l + 1)
                nc.scalar.activation(RR[:], px[:, 0, 0:S], ACT.Sqrt, bias=EPSC[:], scale=1.0 / D
                                     ).then_inc(rms_made, 1)
                split_hi(n0, 2)
                for g in range(4):
                    act.wait_ge(h_made, l * 4 + (g + 1))
                    nc.scalar.copy(Hs[:, 4 * g:4 * g + 4, 0:S], buf(g)[:]).then_inc(h_hi, 1)
                    if g == 0:
                        split_hi(n0, 3)
                act.wait_ge(gate_in, l * 16 + 16)
                nc.scalar.copy(GS[:, :, 0:NG], GW).then_inc(gw_hi, 1)

                def glu_bias(j, half):
                    return lambda t: par(l, j * 2 + (B_CONV + KT * half + t))

                split_and_low(n0, 0, glu_bias(0, 0))
                split_rest(n0, 1, 0, 1)
                act.wait_ge(gates_mm, l + 1)
                nc.scalar.copy(GLOW[:], px[:, 0:ST, NG:2 * NG]).then_inc(gates_low, 1)
                split_rest(n0, 1)
                low_half(n0, 1, glu_bias(0, 1))
                sigmoid_out(n0, 1, QB[:, 2:4, :], glu_sig)
                split_rest(n0, 2, 0, 1)
                act.wait_ge(grows_mm, l + 1)
                nc.scalar.activation(A_R, px[0:2 * H, 2, S:2 * S], ACT.Abs)
                nc.scalar.copy(I_R, px[0:2 * H, 2, 0:S]).then_inc(f_abs, 1)
                act.wait_ge(f_abs, l + 1)
                nc.scalar.activation(A_R, A_R, ACT.Exp, scale=-1.0).then_inc(f_exp, 1)
                act.wait_ge(f_exp, l + 1)
                nc.scalar.activation(A_R, A_R, ACT.Ln, bias=1.0).then_inc(f_log, 1)
                split_rest(n0, 2)
                low_half(n0, 2, glu_bias(1, 0))
                split_rest(n0, 3, 0, 1)
                act.wait_ge(m_made, l + 1)
                nc.scalar.activation(ROWS[:, 1, :], N_R, ACT.Exp).then_inc(rows_made, 1)
                split_rest(n0, 3)
                low_half(n0, 3, glu_bias(1, 1))
                sigmoid_out(n0, 3, QB[:, 2:4, :], glu_sig)
                with act.Fori(2, N_GLU // 2) as j:
                    n = act.snap(l * NP + j * 2)
                    split_and_low(n, 0, glu_bias(j, 0))
                    split_and_low(n, 1, glu_bias(j, 1))
                    sigmoid_out(n, 1, QB[:, 2:4, :], glu_sig)

                split_hi(l * NP + (AT_HEAD + 1), 0)
                with act.Fori(0, H) as h:
                    n = act.snap(l * NP + AT_HEAD + h * 10)
                    u = act.snap(l * H + h)

                    def bias(first):
                        return lambda t: par(l, h * HT + (B_MAIN + first + t))

                    split_rest(n, 0)
                    low_half(n, 0, bias(K_T))
                    for i, first in enumerate((K_T + 2, Q_T, Q_T + 2, V_T)):
                        split_rest(n, i + 1, 0, 1)
                        if i == 0:
                            act.wait_ge(e_ready, u + 1)
                            nc.scalar.activation(EW[:], EW[:], ACT.Exp, scale=-1.0
                                                 ).then_inc(exp_made, 1)
                        act.wait_ge(qk_summed, u * 4 + (i + 1))
                        b = (K_, QB)[i // 2][:, 2 * (i % 2):2 * (i % 2) + 2, :]
                        nc.scalar.activation(b, b, ACT.Silu).then_inc(qk_silu, 1)
                        split_rest(n, i + 1)
                        low_half(n, i + 1, bias(first))
                    split_and_low(n, 5, bias(V_T + 2))
                    split_rest(n, 6, 0, 1)
                    act.wait_ge(dens, u + 1)
                    nc.scalar.activation(R2, px[:, 1, :].rearrange("p (d s) -> p d s", d=2), ACT.Abs
                                         ).then_inc(dens_abs, 1)
                    split_rest(n, 6)
                    low_half(n, 6, bias(O_T))
                    split_rest(n, 7, 0, 1)
                    act.wait_ge(v_turned, u + 1)
                    nc.scalar.copy(VS_, px[:, 2:4, :].rearrange("p a (b c) -> p (a b) c", c=S)
                                   ).then_inc(vs_made, 1)
                    sigmoid_out(n, 6, SO_[:, 0:2, :], o_sig)
                    split_rest(n, 7)
                    low_half(n, 7, bias(O_T + 2))
                    sigmoid_out(n, 7, SO_[:, 2:4, :], o_sig)
                    split_rest(n, 8, 0, 2)
                    act.wait_ge(ht_made, u + 1)
                    nc.scalar.activation(EW[:], KV_, ACT.Square).then_inc(ht_sq, 1)
                    split_rest(n, 8, 2)
                    low_half(n, 8, bias(Z_T))
                    split_rest(n, 9, 0, 1)
                    act.wait_ge(ht_summed, u + 1)
                    nc.scalar.activation(RR[:], px[:, 0, 0:S], ACT.Sqrt, bias=EPSC[:],
                                         scale=1.0 / DH).then_inc(ht_rms, 1)
                    split_rest(n, 9, 1, 2)
                    for i in range(2):
                        if i == 1:
                            split_rest(n, 9, 2)
                            low_half(n, 9, bias(Z_T + 2))
                        act.wait_ge(pairs_out, n + (i + 11))
                        z = QB[:, 2 * i:2 * i + 2, :]
                        nc.scalar.activation(z, z, ACT.Silu).then_inc(z_silu, 1)
                    split_hi(n + 11, 0)
                    act.wait_ge(ya_made, u + 1)
                    nc.scalar.copy(YC[:, ds(h * HT, HT), 0:S], KV_).then_inc(ya_hi, 1)

                with act.Fori(0, N_GA // 2) as j:
                    n = act.snap(l * NP + AT_GA + j * 2)
                    split_rest(n, 0)
                    low_half(n, 0, lambda t: par(l, j * 2 + (B_CONV + 3 * KT + t)))
                    sigmoid_out(n, 0, QB[:, 0:2, :], ga_sig)
                    split_and_low(n, 1)
                    split_hi(n + 3, 0)

                n = act.snap(l * NP + AT_ZB)

                def zb_bias(j):
                    return lambda t: par(l, B_CONV + 2 * KT + 2 * j + t)

                def silu_zb(j):
                    act.wait_ge(pairs_out, n + (j + 3))
                    z = HEAD[:, 2 * j:2 * j + 2, :]
                    nc.scalar.activation(z, z, ACT.Silu).then_inc(zb_silu, 1)

                def square_c(g):
                    if g >= 2:
                        act.wait_ge(c_added, l * 3 + (g - 1))
                    act.wait_ge(centred, l * 4 + (g + 1))
                    nc.scalar.activation(buf(min(g, 1))[:], conv_out(4 * g, 4), ACT.Square
                                         ).then_inc(c_sq, 1)

                def ln_act(g):
                    act.wait_ge(ln_made, l * 4 + (g + 1))
                    for t in range(4):
                        b = buf(g)[:, t, :]
                        i = nc.scalar.activation(b, b, ACT.Silu, scale=par(l, LN_W + 4 * g + t),
                                                 bias=par(l, LN_B + 4 * g + t))
                    i.then_inc(ln_silu, 1)

                def cb_high(g):
                    act.wait_ge(cb_made, l * 4 + (g + 1))
                    nc.scalar.copy(YC[:, 4 * g:4 * g + 4, 0:S], buf(g)[:]).then_inc(cb_hi, 1)

                split_rest(n, 0)
                low_half(n, 0, zb_bias(0))
                split_and_low(n, 1, zb_bias(1))
                split_rest(n, 2, 0, 1)
                for g in range(4):
                    square_c(g)
                split_rest(n, 2)
                low_half(n, 2, zb_bias(2))
                split_rest(n, 3, 0, 1)
                act.wait_ge(c_summed, l + 1)
                nc.scalar.activation(RR[:], px[:, 1, 0:S], ACT.Sqrt, bias=EPSC[:], scale=1.0 / D
                                     ).then_inc(ln_std, 1)
                split_rest(n, 3)
                low_half(n, 3, zb_bias(3))
                for j in range(4):
                    silu_zb(j)
                for g in range(3):
                    split_rest(n, g + 4, 0, 1)
                    ln_act(g)
                    split_rest(n, g + 4, 1, 3)
                    cb_high(g)
                    split_rest(n, g + 4, 3)
                    low_half(n, g + 4, zb_bias(g + 4))
                    silu_zb(g + 4)
                split_rest(n, 7, 0, 1)
                ln_act(3)
                split_rest(n, 7)
                low_half(n, 7, zb_bias(7))
                silu_zb(7)
                cb_high(3)

                def g_b(j, n):
                    split_and_low(n, 0, lambda t: par(l, j * 2 + (B_CONV + 4 * KT + t)))
                    sigmoid_out(n, 0, QB[:, 0:2, :], gb_sig)

                with act.Fori(0, N_GB // 2 - 1) as j:
                    n = act.snap(l * NP + AT_GB + j * 2)
                    g_b(j, n)
                    split_and_low(n, 1)
                n = act.snap(l * NP + (AT_OUT - 2))
                g_b(N_GB // 2 - 1, n)
                act.wait_ge(multiplied, n * QC + 2 * QC)
                for g in range(3):
                    act.wait_ge(m_sum, l * (N_GB // 2) + (2 * g + 3))
                    nc.scalar.copy(Hs[:, 4 * g:4 * g + 4, 0:S], M[:, 4 * g:4 * g + 4, :]
                                   ).then_inc(m_hi, 1)
                    split_hi(n + 2, g)
                low_half(n, 1)
                act.wait_ge(m_sum, l * (N_GB // 2) + (N_GB // 2 + 1))
                nc.scalar.copy(Hs[:, 12:16, 0:S], M[:, 12:16, :]).then_inc(m_hi, 1)
                split_hi(n + 2, 3)

                def out_duo(n, k, d):
                    split_rest(n, k, 0)
                    act.wait_ge(pairs_out, n + (k + 3))
                    square_duo((l + 1) * (KT // 2) + d, d * 2, k)

                with act.Fori(0, N_OUT // 2 - 1) as j:
                    n = act.snap(l * NP + AT_OUT + j * 2)
                    out_duo(n, 0, j * 2)
                    out_duo(n, 1, j * 2 + 1)
                out_duo(act.snap(l * NP + (NP - 2)), 0, N_OUT - 2)

            def weigh(tile):
                nc.scalar.activation(HEAD[:, tile, :], X[:, tile, :], ACT.Identity,
                                     scale=PAR[:, L * PARS + tile:L * PARS + tile + 1]
                                     ).then_inc(y_made, 1)

            for t in range(KT - 2):
                weigh(t)
            act.wait_ge(pairs_out, L * NP + 2)
            square_duo(L * (KT // 2) + (KT // 2 - 1), KT - 2, 1)
            weigh(KT - 2)
            weigh(KT - 1)
            act.wait_ge(summed, L + 1)
            nc.scalar.activation(RR[:, 0:ST], px[:, 0, 0:ST], ACT.Sqrt, bias=EPSC[:], scale=1.0 / D
                                 ).then_inc(rms_made, 1)
            act.wait_ge(inv_made, 1)
            act.wait_ge(y_turned, 1)
            nc.scalar.activation(XROWS[:, 1, :], ps[:].rearrange("p a b -> p (a b)"), ACT.Identity,
                                 scale=RR[:, 1:2]).then_inc(y_rows[1], 1)
        @block.vector
        def _(dve):
            steps = Steps(dve, dve_steps)
            v = nc.vector

            def split_lo(n, c):
                dve.wait_ge(hi_made, n * QC + (c + 1))
                v.tensor_tensor(WL[:, c, :, :], RAW[:, c, :, :], WH[:, c, :, :].bitcast(F32),
                                ALU.subtract).then_inc(lo_made, 1)

            def pair_out(n, k, dst):
                dve.wait_ge(low_out, n + (k + 1))
                q = k % 2
                v.tensor_tensor(dst, ps[:, 2 * q:2 * q + 2, 0:S], T[:, q, :, :], ALU.add
                                ).then_inc(pairs_out, 1)

            def split_next(n, k):
                for c in range(QC):
                    split_lo(n + (k + 1), c)

            v.memset(EPSC[:], EPS)
            v.memset(ONES[:], 1.0).then_inc(ones_made, 1)
            steps.mark(v.memset(ACC[:], 0.0))
            dve.sem_inc(lo_made, QC)
            dve.sem_inc(cb_lo, 1)
            dve.sem_inc(m_sum, 1)
            dve.wait_ge(x_turned, 1)
            steps.mark(v.tensor_copy(X[:, 0:KT // 2, :],
                                     ps[:].rearrange("p a (b c) -> p (a b) c", c=S)))
            steps.wait()
            dve.sem_inc(pairs_out, 2)

            def add_squares(unit, q, first=False):
                dve.wait_ge(squared, unit + 1)
                if not first:
                    dve.wait_ge(sq_added, unit)
                v.tensor_tensor(ACC[:], ACC[:], EW[:, 2 * q:2 * q + 2, :], ALU.add
                                ).then_inc(sq_added, 1)

            for d in range(KT // 2 - 1):
                add_squares(d, d % 2, d == 0)
            dve.wait_ge(par_made, 1)
            dve.wait_ge(x_in, 1)

            def inverse_rms(l):
                dve.wait_ge(rms_made, l + 1)
                steps.mark(v.reciprocal(RR[:], RR[:]))
                steps.wait()

            def scale_x(tile, weight, dst):
                return v.scalar_tensor_tensor(out=dst, in0=X[:, tile, :], scalar=weight, in1=RR[:],
                                              op0=ALU.mult, op1=ALU.mult)

            with dve.Fori(0, L) as l:
                steps.enter(l, LAYER_STEPS)
                n0 = dve.snap(l * NP)

                def norm_group(g):
                    for t in range(4):
                        i = scale_x(4 * g + t, par(l, NORM_W + 4 * g + t), buf(g)[:, t, :])
                    i.then_inc(h_made, 1)

                def h_low(g):
                    dve.wait_ge(h_hi, l * 4 + (g + 1))
                    v.tensor_tensor(Hs[:, 4 * g:4 * g + 4, S:2 * S], buf(g)[:],
                                    Hs[:, 4 * g:4 * g + 4, 0:S].bitcast(F32), ALU.subtract
                                    ).then_inc(h_lo, 1)

                add_squares(l * (KT // 2) + (KT // 2 - 1), 1)
                split_lo(n0, 0)
                split_lo(n0, 1)
                inverse_rms(l)
                norm_group(0)
                split_lo(n0, 2)
                h_low(0)
                norm_group(1)
                split_lo(n0, 3)
                for g in range(1, 4):
                    h_low(g)
                    if g < 3:
                        dve.wait_ge(h_lo, l * 4 + g)
                        norm_group(g + 1)
                dve.wait_ge(gate_in, l * 16 + 16)
                dve.wait_ge(gw_hi, l + 1)
                v.tensor_tensor(GS[:, :, NG:2 * NG], GW, GS[:, :, 0:NG].bitcast(F32), ALU.subtract
                                ).then_inc(gw_lo, 1)

                taps = [k for k in range(DW_TAPS) if k != PAD] + [PAD]

                def conv_begin(tile):
                    steps.wait()
                    for t in range(2):
                        steps.mark(v.tensor_copy(CWT[:, t, 0:DW_TAPS],
                                                 par(l, tile + (DW_W + t), DW_TAPS, KT)))
                        steps.mark(v.tensor_copy(CWT[:, t, DW_TAPS:DW_TAPS + 1],
                                                 par(l, tile + (DW_B + t))))

                def conv_taps(tile, first, last):
                    for i in range(first, last):
                        k = taps[i]
                        for t in range(2):
                            steps.wait(1)
                            src, w = conv_in(tile + t, k), CWT[:, t, k:k + 1]
                            if i == 0:
                                steps.mark(v.tensor_scalar(ACC[:, t, :], src, w,
                                                           CWT[:, t, DW_TAPS:DW_TAPS + 1],
                                                           ALU.mult, ALU.add))
                            else:
                                dst = src if k == PAD else ACC[:, t, :]
                                steps.mark(v.scalar_tensor_tensor(
                                    out=dst, in0=src, scalar=w, in1=ACC[:, t, :],
                                    op0=ALU.mult, op1=ALU.add))

                def glu_mul(tile, unit):
                    dve.wait_ge(glu_sig, unit)
                    dst = CP[:, ds(tile * CW, 2 * CW)].rearrange("p (t c) -> p t c", c=CW)
                    steps.mark(v.tensor_tensor(dst[:, :, PAD:CW], QB[:, 0:2, :], QB[:, 2:4, :],
                                               ALU.mult))

                split_next(n0, 0)
                pair_out(n0, 0, QB[:, 0:2, :])
                split_lo(n0 + 2, 0)
                dve.wait_ge(gates_low, l + 1)
                dve.wait_ge(pads_made, 1)
                steps.mark(v.tensor_tensor(GLOW[:], GLOW[:],
                                           GBIAS[:, ds(l, 1), :].to_broadcast([P, ST, NG]), ALU.add))
                steps.wait()
                for group, (kind, row) in enumerate(((0, 0), (2, 0), (1, H), (3, H))):
                    g = slice(H * group, H * group + H)
                    i = v.tensor_tensor(GC[:, :, kind, row:row + H], px[:, 0:ST, g], GLOW[:, :, g],
                                        ALU.add)
                i.then_inc(gcols_made, 1)
                for c in range(1, QC):
                    split_lo(n0 + 2, c)
                pair_out(n0, 1, QB[:, 2:4, :])
                glu_mul(0, l * (N_GLU // 2) + 1)
                split_lo(n0 + 3, 0)
                dve.wait_ge(f_abs, l + 1)
                steps.mark(v.tensor_scalar(F_R, px[0:2 * H, 2, S:2 * S], 0.0, None, ALU.min))
                steps.mark(v.memset(Z_R, 0.0))
                steps.wait()
                dve.wait_ge(f_log, l + 1)
                steps.mark(v.tensor_tensor(F_R, F_R, A_R, ALU.subtract))
                steps.wait()
                steps.mark(v.tensor_tensor_scan(G_R, F_R, Z_R, 0.0, ALU.add, ALU.add))
                steps.wait()
                steps.mark(v.tensor_tensor(C_R, I_R, G_R, ALU.subtract))
                steps.wait()
                steps.mark(v.tensor_tensor_scan(ROWS[:, 0, :], C_R, C_R, 0.0, ALU.max, ALU.max))
                steps.mark(v.tensor_copy(CB_R, C_R[:, ::-1]))
                steps.wait(1)
                steps.mark(v.scalar_tensor_tensor(out=N_R, in0=G_R, scalar=-1.0, in1=ROWS[:, 0, :],
                                                  op0=ALU.mult, op1=ALU.subtract))
                steps.wait()
                v.tensor_scalar(N_R, N_R, EXP_CAP, None, ALU.min).then_inc(m_made, 1)
                for c in range(1, QC):
                    split_lo(n0 + 3, c)
                pair_out(n0, 2, QB[:, 0:2, :])
                split_next(n0, 3)
                pair_out(n0, 3, QB[:, 2:4, :])
                dve.wait_ge(ccol_mm, l + 1)
                cc = px[:, 3, 0:4 * ST * H].rearrange("p (s c) -> p s c", s=ST)
                steps.mark(v.tensor_copy(CCOL[:, :, 0:H], cc[:, :, 0:H]))
                steps.mark(v.tensor_copy(CCOL[:, :, H:2 * H], cc[:, :, 3 * H:4 * H]))
                glu_mul(2, l * (N_GLU // 2) + 2)

                with dve.Fori(0, 2) as i:
                    steps.enter(i, 3 + 4 + 2 * DW_TAPS)
                    n = dve.snap(l * NP + 4 + i * 6)
                    duo = dve.snap(i * 2)
                    conv_begin(duo)
                    for j in range(3):
                        for k, dst, first, last in ((2 * j, QB[:, 0:2, :], 10 * j, 10 * j + 5),
                                                    (2 * j + 1, QB[:, 2:4, :], 10 * j + 5,
                                                     10 * j + 10 + j // 2)):
                            split_lo(n + (k + 1), 0)
                            conv_taps(duo, first, first + 2)
                            split_lo(n + (k + 1), 1)
                            conv_taps(duo, first + 2, first + 4)
                            split_lo(n + (k + 1), 2)
                            conv_taps(duo, first + 4, last)
                            split_lo(n + (k + 1), 3)
                            pair_out(n, k, dst)
                        glu_mul(i * 6 + (4 + 2 * j), l * (N_GLU // 2) + i * 3 + (3 + j))
                    steps.leave(2)

                split_lo(l * NP + (AT_HEAD + 1), 0)
                with dve.Fori(0, H) as h:
                    steps.enter(h, HEAD_STEPS)
                    n = dve.snap(l * NP + AT_HEAD + h * 10)
                    u = dve.snap(l * H + h)
                    duo = dve.snap(h * 2 + 4)

                    def with_taps(k, a, b, first=0):
                        cut = [a + (b - a) * c // 3 for c in range(4)]
                        for c in range(first, QC):
                            split_lo(n + (k + 1), c)
                            if c < 3:
                                conv_taps(duo, cut[c], cut[c + 1])

                    def narrow_conv(i, dst, first):
                        dve.wait_ge(pairs_out, n + (i + 3))
                        for tap in range(QK_TAPS):
                            for t in range(2):
                                src = QPAD[:, t, tap:tap + S]
                                w = par(l, h * HT + (QK_W + tap * 2 * KT + first + t))
                                if tap == 0:
                                    steps.mark(v.tensor_scalar(dst[:, t, :], src, w, None, ALU.mult))
                                    continue
                                steps.wait(1)
                                ins = v.scalar_tensor_tensor(out=dst[:, t, :], in0=src, scalar=w,
                                                             in1=dst[:, t, :], op0=ALU.mult,
                                                             op1=ALU.add)
                                if tap == QK_TAPS - 1 and t == 1:
                                    ins.then_inc(qk_summed, 1)
                                else:
                                    steps.mark(ins)

                    def one_head_rows(which):
                        v.tensor_scalar(RS[:, 0, :], ROWS[:, which, :], IDENT[0:2 * H, ds(h, 1)],
                                        None, ALU.mult)
                        v.tensor_scalar(RS[:, 1, :], ROWS[:, which, ::-1],
                                        IDENT[0:2 * H, ds(h + H, 1)], None, ALU.mult
                                        ).then_inc(rs_made, 1)

                    conv_begin(duo)
                    one_head_rows(0)
                    with_taps(0, 0, 1, 1)
                    pair_out(n, 0, QPAD[:, :, 2:2 + S])
                    dve.wait_ge(m_spread, u + 1)
                    for d in range(2):
                        for st in range(ST):
                            i = v.tensor_scalar(EW[:, 2 * d + st, :], px[:, 1, d * S:(d + 1) * S],
                                                CCOL[:, st, ds(h + d * H, 1)], 0.0,
                                                ALU.subtract, ALU.max)
                    i.then_inc(e_ready, 1)
                    narrow_conv(0, K_[:, 0:2, :], KT)
                    with_taps(1, 1, 1)
                    dve.wait_ge(qk_summed, u * 4 + 1)
                    pair_out(n, 1, QPAD[:, :, 2:2 + S])
                    narrow_conv(1, K_[:, 2:4, :], KT + 2)
                    with_taps(2, 1, 2)
                    dve.wait_ge(qk_summed, u * 4 + 2)
                    pair_out(n, 2, QPAD[:, :, 2:2 + S])
                    narrow_conv(2, QB[:, 0:2, :], 0)
                    with_taps(3, 2, 3)
                    dve.wait_ge(qk_summed, u * 4 + 3)
                    pair_out(n, 3, QPAD[:, :, 2:2 + S])
                    narrow_conv(3, QB[:, 2:4, :], 2)
                    with_taps(4, 3, 9)
                    pair_out(n, 4, V_[:, 0:2, :])
                    split_lo(n + 6, 0)
                    conv_taps(duo, 9, 11)
                    split_lo(n + 6, 1)
                    split_lo(n + 6, 2)
                    dve.wait_ge(scores, u + 1)
                    sc = px[:, 0, :].rearrange("p (a b) -> p a b", a=ST)
                    for d in range(2):
                        dve.wait_ge(masked, u * 2 + (d + 1))
                        i = v.scalar_tensor_tensor(out=QB[:, 2 * d:2 * d + 2, :], in0=sc,
                                                   scalar=float(DH) ** -0.5,
                                                   in1=EW[:, 2 * d:2 * d + 2, :],
                                                   op0=ALU.mult, op1=ALU.mult)
                    i.then_inc(pw_made, 1)
                    dve.wait_ge(pw_made, u + 1)
                    dve.wait_ge(rows_made, l + 1)
                    one_head_rows(1)
                    conv_taps(duo, 11, 15)
                    split_lo(n + 6, 3)
                    pair_out(n, 5, V_[:, 2:4, :])
                    split_lo(n + 7, 0)
                    dve.wait_ge(e_spread, u + 1)
                    dve.wait_ge(dens_abs, u + 1)
                    steps.mark(v.tensor_tensor(R2, R2, px[:, 0, :].rearrange("p (a b) -> p a b", a=2),
                                               ALU.max))
                    steps.wait()
                    steps.mark(v.reciprocal(R2[:, 0, :], R2[:, 0, :]))
                    split_lo(n + 7, 1)
                    steps.mark(v.reciprocal(R2[:, 1, :], R2[:, 1, :]))
                    split_lo(n + 7, 2)
                    steps.wait(1)
                    steps.mark(v.tensor_tensor(QB[:, 0:2, :], QB[:, 0:2, :],
                                               spread(R2[:, 0, :], 2), ALU.mult))
                    steps.wait(1)
                    steps.mark(v.tensor_tensor(QB[:, 2:4, :], QB[:, 2:4, :],
                                               spread(R2[:, 1, :], 2), ALU.mult))
                    split_lo(n + 7, 3)
                    steps.wait()
                    v.tensor_tensor(QB[:, 0:2, :], QB[:, 0:2, :], QB[:, 2:4, :], ALU.add
                                    ).then_inc(a_made, 1)
                    pair_out(n, 6, SO_[:, 0:2, :])
                    with_taps(7, 15, 23)
                    pair_out(n, 7, SO_[:, 2:4, :])
                    split_lo(n + 9, 0)
                    dve.wait_ge(ht_mm, u + 1)
                    dve.wait_ge(o_sig, u * 2 + 2)
                    v.tensor_tensor(KV_, px[:, 2:4, :].rearrange("p a (b c) -> p (a b) c", c=S), SO_,
                                    ALU.mult).then_inc(ht_made, 1)
                    split_lo(n + 9, 1)
                    conv_taps(duo, 23, 26)
                    split_lo(n + 9, 2)
                    conv_taps(duo, 26, 29)
                    split_lo(n + 9, 3)
                    pair_out(n, 8, QB[:, 0:2, :])
                    split_lo(n + 10, 0)
                    dve.wait_ge(ht_rms, u + 1)
                    steps.mark(v.reciprocal(RR[:], RR[:]))
                    steps.wait()
                    split_lo(n + 10, 1)
                    conv_taps(duo, 29, DW_TAPS)
                    steps.mark(v.tensor_tensor(KV_, KV_, spread(RR[:], HT), ALU.mult))
                    split_lo(n + 10, 2)
                    split_lo(n + 10, 3)
                    pair_out(n, 9, QB[:, 2:4, :])
                    steps.wait()
                    for t in range(HT):
                        if t % 2 == 0:
                            dve.wait_ge(z_silu, u * 2 + (t // 2 + 1))
                        i = v.scalar_tensor_tensor(out=KV_[:, t, :], in0=KV_[:, t, :],
                                                   scalar=par(l, h * HT + (MNORM_W + t)),
                                                   in1=QB[:, t, :], op0=ALU.mult, op1=ALU.mult)
                    i.then_inc(ya_made, 1)
                    split_lo(n + 11, 0)
                    dve.wait_ge(ya_hi, u + 1)
                    v.tensor_tensor(YC[:, ds(h * HT, HT), S:2 * S], KV_,
                                    YC[:, ds(h * HT, HT), 0:S].bitcast(F32), ALU.subtract
                                    ).then_inc(ya_lo, 1)
                    steps.leave(H)

                with dve.Fori(0, 2) as i:
                    steps.enter(i, 4 + 4 + 2 * DW_TAPS)
                    n = dve.snap(l * NP + AT_GA + i * 8)
                    duo = dve.snap(i * 2 + 12)
                    conv_begin(duo)
                    for j in range(4):
                        for k, dst in ((2 * j, QB[:, 0:2, :]), (2 * j + 1, QB[:, 2:4, :])):
                            if k % 2 == 1:
                                split_lo(n + (k + 1), 0)
                            split_lo(n + (k + 1), 1)
                            conv_taps(duo, 4 * k, 4 * k + 2)
                            split_lo(n + (k + 1), 2)
                            conv_taps(duo, 4 * k + 2, min(4 * k + 4, DW_TAPS))
                            split_lo(n + (k + 1), 3)
                            pair_out(n, k, dst)
                        split_lo(n + (2 * j + 3), 0)
                        dve.wait_ge(pairs_out, n + (2 * j + 4))
                        dve.wait_ge(ga_sig, l * (N_GA // 2) + i * 4 + (j + 1))
                        steps.mark(v.tensor_tensor(M[:, ds(i * 8 + 2 * j, 2), :], QB[:, 0:2, :],
                                                   QB[:, 2:4, :], ALU.mult))
                    steps.leave(2)
                n = dve.snap(l * NP + AT_ZB)

                def scale_c(g):
                    v.tensor_tensor(buf(g)[:], conv_out(4 * g, 4), spread(RR[:], 4), ALU.mult
                                    ).then_inc(ln_made, 1)

                def gate_c(g):
                    dve.wait_ge(ln_silu, l * 4 + (g + 1))
                    dve.wait_ge(zb_silu, l * N_ZB + (2 * g + 2))
                    v.tensor_tensor(buf(g)[:], buf(g)[:], HEAD[:, 4 * g:4 * g + 4, :], ALU.mult
                                    ).then_inc(cb_made, 1)

                def low_c(g):
                    dve.wait_ge(cb_hi, l * 4 + (g + 1))
                    v.tensor_tensor(YC[:, 4 * g:4 * g + 4, S:2 * S], buf(g)[:],
                                    YC[:, 4 * g:4 * g + 4, 0:S].bitcast(F32), ALU.subtract
                                    ).then_inc(cb_lo, 1)

                for g in range(1, 4):
                    split_lo(n + 1, g)
                    steps.wait()
                    steps.mark(v.tensor_tensor(EW[:], conv_out(0, 4) if g == 1 else EW[:],
                                               conv_out(4 * g, 4), ALU.add))
                steps.wait()
                dve.sem_inc(conv_made, 1)
                pair_out(n, 0, HEAD[:, 0:2, :])
                split_lo(n + 2, 0)
                dve.wait_ge(mean_mm, l + 1)
                steps.mark(v.tensor_scalar(RR[:], px[:, 0, 0:S], 1.0 / D, None, ALU.mult))
                steps.wait()
                for g in range(4):
                    v.tensor_tensor(conv_out(4 * g, 4), conv_out(4 * g, 4), spread(RR[:], 4),
                                    ALU.subtract).then_inc(centred, 1)
                    if g < 3:
                        split_lo(n + 2, g + 1)
                pair_out(n, 1, HEAD[:, 2:4, :])
                split_lo(n + 3, 0)
                for g in range(1, 4):
                    dve.wait_ge(c_sq, l * 4 + (g + 1))
                    if g > 1:
                        dve.wait_ge(c_added, l * 3 + (g - 1))
                    v.tensor_tensor(EW[:], EW[:], QB[:], ALU.add).then_inc(c_added, 1)
                for c in range(1, QC):
                    split_lo(n + 3, c)
                pair_out(n, 2, HEAD[:, 4:6, :])
                split_lo(n + 4, 0)
                dve.wait_ge(ln_std, l + 1)
                steps.mark(v.reciprocal(RR[:], RR[:]))
                split_lo(n + 4, 1)
                steps.wait()
                scale_c(0)
                split_lo(n + 4, 2)
                split_lo(n + 4, 3)
                pair_out(n, 3, HEAD[:, 6:8, :])
                for g in range(3):
                    split_lo(n + (g + 5), 0)
                    gate_c(g)
                    split_lo(n + (g + 5), 1)
                    if g > 0:
                        dve.wait_ge(cb_lo, l * 4 + (g + 1))
                    scale_c(g + 1)
                    split_lo(n + (g + 5), 2)
                    dve.wait_ge(cb_made, l * 4 + (g + 1))
                    low_c(g)
                    split_lo(n + (g + 5), 3)
                    pair_out(n, g + 4, HEAD[:, 2 * g + 8:2 * g + 10, :])
                split_next(n, 7)
                pair_out(n, 7, HEAD[:, 14:16, :])
                gate_c(3)
                dve.wait_ge(cb_made, l * 4 + 4)
                low_c(3)

                def add_b(tile, unit, n, k):
                    dve.wait_ge(pairs_out, n + (k + 3))
                    dve.wait_ge(gb_sig, unit)
                    steps.mark(v.tensor_tensor(QB[:, 2:4, :], QB[:, 0:2, :], QB[:, 2:4, :],
                                               ALU.mult))
                    steps.wait()
                    m = M[:, ds(tile, 2), :]
                    v.tensor_tensor(m, m, QB[:, 2:4, :], ALU.add).then_inc(m_sum, 1)

                with dve.Fori(0, N_GB // 2 - 1) as j:
                    steps.enter(j, 1)
                    n = dve.snap(l * NP + AT_GB + j * 2)
                    split_next(n, 0)
                    dve.wait_ge(cb_lo, l * 4 + 5)
                    dve.wait_ge(m_sum, l * (N_GB // 2) + j + 1)
                    pair_out(n, 0, QB[:, 0:2, :])
                    split_next(n, 1)
                    pair_out(n, 1, QB[:, 2:4, :])
                    add_b(j * 2, l * (N_GB // 2) + j + 1, n, 1)
                    steps.leave(N_GB // 2 - 1)
                n = dve.snap(l * NP + AT_OUT)

                def merged_low(g):
                    dve.wait_ge(m_hi, l * 4 + (g + 1))
                    v.tensor_tensor(Hs[:, 4 * g:4 * g + 4, S:2 * S], M[:, 4 * g:4 * g + 4, :],
                                    Hs[:, 4 * g:4 * g + 4, 0:S].bitcast(F32), ALU.subtract
                                    ).then_inc(m_lo, 1)

                split_next(n - 2, 0)
                dve.wait_ge(m_sum, l * (N_GB // 2) + N_GB // 2)
                pair_out(n - 2, 0, QB[:, 0:2, :])
                for g in range(3):
                    merged_low(g)
                    split_lo(n, g)
                pair_out(n - 2, 1, QB[:, 2:4, :])
                add_b(KT - 2, l * (N_GB // 2) + N_GB // 2, n - 2, 1)
                steps.mark(v.memset(ACC[:], 0.0))
                merged_low(3)
                steps.wait()
                split_lo(n, 3)

                def add_x(tile, n, k):
                    xt, q = X[:, ds(tile, 2), :], k % 2
                    dve.wait_ge(multiplied, n * QC + (k + 2) * QC)
                    v.tensor_tensor(xt, xt, ps[:, 2 * q:2 * q + 2, S:2 * S], ALU.add
                                    ).then_inc(low_out, 1)
                    dve.wait_ge(low_out, n + (k + 1))
                    v.tensor_tensor(xt, xt, ps[:, 2 * q:2 * q + 2, 0:S], ALU.add
                                    ).then_inc(pairs_out, 1)

                unit = dve.snap(l * (KT // 2) + KT // 2)

                with dve.Fori(0, N_OUT // 2 - 1) as j:
                    n = dve.snap(l * NP + AT_OUT + j * 2)
                    for k in range(2):
                        split_next(n, k)
                        add_x(j * 4 + 2 * k, n, k)
                        add_squares(unit + j * 2 + k, k)
                n = dve.snap(l * NP + NP - 2)
                split_next(n, 0)
                add_x(KT - 4, n, 0)
                add_squares(unit + (N_OUT - 2), 0)
                add_x(KT - 2, n, 1)
                steps.leave(L)

            add_squares(L * (KT // 2) + (KT // 2 - 1), 1)
            dve.wait_ge(rms_made, L + 1)
            v.reciprocal(RR[:, 0:ST], RR[:, 0:ST]).then_inc(inv_made, 1)
            dve.wait_ge(inv_made, 1)
            dve.wait_ge(y_turned, 2)
            v.tensor_scalar(XROWS[:, 0, :], px[:].rearrange("p a b -> p (a b)"), RR[:, 0:1], None,
                            ALU.mult).then_inc(y_rows[0], 1)

        @block.tensor
        def _(pe):
            mm = nc.tensor.matmul

            def multiply(n, k, act_in, made=None, base=0):
                q = k % 2
                for c in range(QC):
                    if made is not None:
                        pe.wait_ge(made, base + (c + 1))
                    pe.wait_ge(lo_made, n * QC + (k * QC + QC + c + 1))
                    if c == 0:
                        pe.wait_ge(pairs_out, n + (k + 1))
                    for kk in range(KQ):
                        kt = c * KQ + kk
                        for t in range(2):
                            bank, cols = ps[:, 2 * q + t, :], slice(t * P, t * P + P)
                            mm(bank, WH[:, c, kk, cols], act_in[:, kt, :], start=(kt == 0), stop=False)
                            i = mm(bank[:, S:2 * S], WL[:, c, kk, cols], act_in[:, kt, 0:S],
                                   start=False, stop=(kt == KT - 1))
                    i.then_inc(multiplied, 1)

            pe.sem_inc(multiplied, QC)
            pe.wait_ge(ident_made, 1)
            pe.wait_ge(x_rows_in, 16)
            for half, bank in enumerate((ps, px)):
                for t in range(KT // 2):
                    for s in range(ST):
                        at = (t % 2) * S + s * P
                        tile = half * (KT // 2) + t
                        i = nc.tensor.transpose(bank[:, t // 2, at:at + P],
                                                XROWS[:, s, tile * P:(tile + 1) * P], IDENT[:])
                i.then_inc(x_turned, 1)
            pe.wait_ge(rows_in, 16 * len(row_loads))
            pe.wait_ge(x_in, 1)
            for b in range(L * PBLK + 1):
                rows = P if b < L * PBLK else KT
                i = nc.tensor.transpose(px[:, b // 4, (b % 4) * P:(b % 4) * P + rows],
                                        PROWS[0:rows, b, :], IDENT[0:rows, 0:rows])
            i.then_inc(rows_turned, 1)
            pe.wait_ge(ones_made, 1)
            pe.wait_ge(par_made, 1)

            def sum_channels(bank, tiles, done):
                for t, tile in enumerate(tiles):
                    i = mm(px[:, bank, 0:S], ONES[:], tile, start=(t == 0),
                           stop=(t == len(tiles) - 1))
                i.then_inc(done, 1)

            with pe.Fori(0, L) as l:
                n0 = pe.snap(l * NP)
                pe.wait_ge(sq_added, l * (KT // 2) + KT // 2)
                sum_channels(0, [ACC[:, t, :] for t in range(2)], summed)
                multiply(n0, 0, Hs, h_lo, l * 4)

                pe.wait_ge(gw_lo, l + 1)
                for k in range(KT):
                    for s in range(ST):
                        mm(px[:, s, 0:2 * NG], Hs[:, k, s * P:(s + 1) * P], GS[:, k, 0:2 * NG],
                           start=(k == 0), stop=False)
                        i = mm(px[:, s, NG:2 * NG], Hs[:, k, S + s * P:S + (s + 1) * P],
                               GS[:, k, 0:NG], start=False, stop=(k == KT - 1))
                i.then_inc(gates_mm, 1)
                multiply(n0, 1, Hs)
                pe.wait_ge(gcols_made, l + 1)
                for kind in range(2):
                    for s in range(ST):
                        dst = px[0:2 * H, 2, kind * S + s * P:kind * S + (s + 1) * P]
                        mm(dst, GC[:, s, 2 * kind, :], IDENT[:], start=True, stop=False)
                        i = mm(dst, GC[:, ST - 1 - s, 2 * kind + 1, :], IDENT[:, ::-1],
                               start=False, stop=True)
                i.then_inc(grows_mm, 1)
                multiply(n0, 2, Hs)
                multiply(n0, 3, Hs)
                pe.wait_ge(m_made, l + 1)
                for s in range(ST):
                    for b, rows in enumerate((C_R, CB_R)):
                        at = s * 4 * H + b * 2 * H
                        i = mm(px[:, 3, at:at + 2 * H], rows[:, s * P:(s + 1) * P],
                               IDENT[0:2 * H, 0:2 * H], start=True, stop=True)
                i.then_inc(ccol_mm, 1)
                with pe.Fori(2, N_GLU // 2) as j:
                    n = pe.snap(l * NP + j * 2)
                    multiply(n, 0, Hs)
                    multiply(n, 1, Hs)

                with pe.Fori(0, H) as h:
                    n = pe.snap(l * NP + AT_HEAD + h * 10)
                    u = pe.snap(l * H + h)

                    def spread_rows(bank):
                        for d in range(2):
                            i = mm(px[:, bank, d * S:(d + 1) * S], ONES[0:2 * H, :], RS[:, d, :],
                                   start=True, stop=True)
                        return i

                    multiply(n, 0, Hs)
                    pe.wait_ge(rs_made, u * 2 + 1)
                    spread_rows(1).then_inc(m_spread, 1)
                    for k in range(1, 5):
                        multiply(n, k, Hs)
                    pe.wait_ge(qk_silu, u * 4 + 4)
                    for s in range(ST):
                        for k in range(HT):
                            i = mm(px[:, 0, s * S:(s + 1) * S], K_[:, k, s * P:(s + 1) * P],
                                   QB[:, k, :], start=(k == 0), stop=(k == HT - 1))
                    i.then_inc(scores, 1)
                    multiply(n, 5, Hs)
                    pe.wait_ge(pw_made, u + 1)
                    for d in range(2):
                        for s in range(ST):
                            i = mm(px[:, 1, d * S:(d + 1) * S], ONES[:], QB[:, 2 * d + s, :],
                                   start=(s == 0), stop=(s == ST - 1))
                    i.then_inc(dens, 1)
                    pe.wait_ge(rs_made, u * 2 + 2)
                    spread_rows(0).then_inc(e_spread, 1)
                    multiply(n, 6, Hs)
                    pe.wait_ge(pairs_out, n + 8)
                    for s in range(ST):
                        for k in range(HT):
                            i = nc.tensor.transpose(px[:, 2 + s, k * P:(k + 1) * P],
                                                    V_[:, k, s * P:(s + 1) * P], IDENT[:])
                    i.then_inc(v_turned, 1)
                    multiply(n, 7, Hs)
                    pe.wait_ge(a_made, u + 1)
                    pe.wait_ge(vs_made, u + 1)
                    vs = VS_.rearrange("p (s a) b -> p s (a b)", s=ST)
                    for k in range(HT):
                        for s in range(ST):
                            i = mm(px[:, 2 + k // 2, (k % 2) * S:(k % 2 + 1) * S],
                                   vs[:, s, k * P:(k + 1) * P], QB[:, s, :],
                                   start=(s == 0), stop=(s == ST - 1))
                    i.then_inc(ht_mm, 1)
                    multiply(n, 8, Hs)
                    pe.wait_ge(ht_sq, u + 1)
                    for t in range(HT):
                        i = mm(px[:, 0, 0:S], ONES[:], EW[:, t, :], start=(t == 0), stop=(t == HT - 1))
                    i.then_inc(ht_summed, 1)
                    multiply(n, 9, Hs)

                with pe.Fori(0, N_GA // 2) as j:
                    n = pe.snap(l * NP + AT_GA + j * 2)
                    multiply(n, 0, Hs)
                    pe.wait_ge(ya_lo, l * H + H)
                    multiply(n, 1, YC)

                n = pe.snap(l * NP + AT_ZB)
                multiply(n, 0, Hs)
                pe.wait_ge(conv_made, l + 1)
                sum_channels(0, [EW[:, t, :] for t in range(4)], mean_mm)
                multiply(n, 1, Hs)
                multiply(n, 2, Hs)
                pe.wait_ge(c_added, l * 3 + 3)
                sum_channels(1, [EW[:, t, :] for t in range(4)], c_summed)
                multiply(n, 3, Hs)
                with pe.Fori(2, N_ZB // 2) as j:
                    n = pe.snap(l * NP + AT_ZB + j * 2)
                    multiply(n, 0, Hs)
                    multiply(n, 1, Hs)

                with pe.Fori(0, N_GB // 2) as j:
                    n = pe.snap(l * NP + AT_GB + j * 2)
                    multiply(n, 0, Hs)
                    pe.wait_ge(cb_lo, l * 4 + 5)
                    multiply(n, 1, YC)
                with pe.Fori(0, N_OUT // 2) as j:
                    n = pe.snap(l * NP + AT_OUT + j * 2)
                    multiply(n, 0, Hs, m_lo, l * 4)
                    multiply(n, 1, Hs)

            def turn(s, bank, tiles):
                for t in tiles:
                    i = nc.tensor.transpose(bank[:, t // 4, (t % 4) * P:(t % 4 + 1) * P],
                                            HEAD[:, t, s * P:(s + 1) * P], IDENT[:])
                return i

            pe.wait_ge(y_made, KT - 2)
            turn(0, px, range(4, KT - 2))
            pe.wait_ge(pairs_out, L * NP + 1)
            turn(1, ps, range(KT // 2))
            pe.wait_ge(sq_added, (L + 1) * (KT // 2))
            for s in range(ST):
                for t in range(2):
                    i = mm(px[:, 0, s:s + 1], ACC[:, t, s * P:(s + 1) * P], ONES[:, 0:1],
                           start=(t == 0), stop=(t == 1))
            i.then_inc(summed, 1)
            turn(1, ps, range(KT // 2, KT - 2))
            pe.wait_ge(y_made, KT)
            turn(0, px, range(KT - 2, KT))
            turn(1, ps, range(KT - 2, KT)).then_inc(y_turned, 1)
            pe.wait_ge(rms_made, L + 1)
            turn(0, px, range(4)).then_inc(y_turned, 1)


_INS = ["x", "norm_w", "w_in", "b_in", "qk_conv_w", "mlstm_norm_w", "w_a", "dw_w", "dw_b",
        "ln_w", "ln_b", "w_b", "w_out", "final_norm_w"]
_OUT = ((1, S, D), "float32")


def kernel(**inputs):
    import numpy as _np
    import concourse.bacc as _bacc
    from concourse import mybir as _mybir
    from concourse.bass_utils import run_bass_kernel_spmd as _run

    nc = _bacc.Bacc("TRN2", target_bir_lowering=False, num_devices=1)
    arrays, args = {}, []
    for name in _INS:
        a = _np.ascontiguousarray(inputs[name])
        arrays[f"in_{name}_dram"] = a
        args.append(nc.dram_tensor(f"in_{name}_dram", a.shape, _mybir.dt.from_np(a.dtype),
                                   kind="ExternalInput").ap())
    dt = _mybir.dt.from_np(_np.dtype(_OUT[1]))
    args.append(nc.dram_tensor("out_0_dram", _OUT[0], dt, kind="ExternalOutput").ap())
    build_trunk(nc, *args)
    r = _run(nc, [arrays], core_ids=[0])
    return r.results[0]["out_0_dram"]
```

```python
from contextlib import ExitStack

import concourse.bass as bass
from concourse import mybir

F32 = mybir.dt.float32
F32R = mybir.dt.float32r
ALU = mybir.AluOpType
ACT = mybir.ActivationFunctionType
ds = bass.ds

P = 128
L = 2
D = 2048
S = 256
ST = S // P
KT = D // P
H = 4
HT = KT // H
DH = D // H
QK_TAPS = 5
DW_TAPS = 31
PAD = DW_TAPS // 2
CW = S + PAD
EPS = 1e-6
NG = 4 * H
GATE0 = 5 * D
GLU_A, GLU_B, Z_B, G_A, G_B = (GATE0 + NG + i * D for i in range(5))
EXP_CAP = 88.0

QC = 4
KQ = KT // QC
PC = 2 * P
N_GLU, N_HEAD, N_GA, N_ZB, N_GB, N_OUT = KT, 10 * H, KT, KT // 2, KT, KT // 2
AT_GLU = 0
AT_HEAD = AT_GLU + N_GLU
AT_GA = AT_HEAD + N_HEAD
AT_ZB = AT_GA + N_GA
AT_GB = AT_ZB + N_ZB
AT_OUT = AT_GB + N_GB
NP = AT_OUT + N_OUT

NORM_W = 0
B_MAIN, B_CONV = KT, 6 * KT
QK_W = 11 * KT
DW_W = QK_W + QK_TAPS * 2 * KT
MNORM_W, DW_B, LN_W, LN_B = (DW_W + (DW_TAPS + i) * KT for i in range(4))
PARS = LN_B + KT
PBLK = PARS // P
assert PBLK * P == PARS
Q_T, K_T, V_T, O_T, Z_T = (i * KT for i in range(5))

Y_SPLIT = 10

HEAD_STEPS = 108
LAYER_STEPS = 739


class Steps:

    def __init__(self, eng, sem):
        self.eng, self.sem, self.base, self.k, self.outer = eng, sem, 0, 0, []

    def mark(self, instruction):
        instruction.then_inc(self.sem, 1)
        self.k += 1

    def wait(self, back=0):
        self.eng.wait_ge(self.sem, self.base + (self.k - back))

    def enter(self, index, per):
        self.outer.append((self.base, self.k, per))
        self.base, self.k = self.eng.snap(self.base + index * per + self.k), 0

    def leave(self, rounds):
        base, k, per = self.outer.pop()
        assert self.k == per, (self.k, per)
        self.base, self.k = base, k + rounds * per


def build_trunk(nc, x, norm_w, w_in, b_in, qk_conv_w, mlstm_norm_w, w_a, dw_w, dw_b,
                ln_w, ln_b, w_b, w_out, final_norm_w, out):
    with ExitStack() as ctx:
        def sb(name, shape, dt=F32):
            return ctx.enter_context(nc.sbuf_tensor(name, shape, dt))

        def sem(name):
            return ctx.enter_context(nc.semaphore(name))

        X = sb("X", [P, KT, S])
        Hs = sb("Hs", [P, KT, 2 * S], F32R)
        YC = sb("YC", [P, KT, 2 * S], F32R)
        CP = sb("CP", [P, KT * CW + PAD])
        M = sb("M", [P, KT, S])
        HEAD = sb("HEAD", [P, KT, S])
        QB = sb("QB", [P, HT, S])
        EW = sb("EW", [P, HT, S])
        QPAD = sb("QPAD", [P, 2, S + QK_TAPS - 1])
        T = sb("T", [P, 2, 2, S])
        ROWS = sb("ROWS", [2 * H, 2, S])
        ACC = sb("ACC", [P, 2, S])
        CWT = sb("CWT", [P, 2, DW_TAPS + 1])
        RR = sb("RR", [P, S])
        RAW = sb("RAW", [P, QC, KQ, PC])
        W = sb("W", [P, QC, 2, KQ, PC], F32R)
        PAR = sb("PAR", [P, L * PARS + KT])
        IDENT = sb("IDENT", [P, P])
        ONES = sb("ONES", [P, P])
        GBIAS = sb("GBIAS", [NG, L])
        GC = sb("GC", [P, ST, 4, 2 * H])
        CCOL = sb("CCOL", [P, ST, 2 * H])
        ECOL = sb("ECOL", [P, 2, H, ST])
        R4 = sb("R4", [P, 2 * ST])[:]
        EPSC = sb("EPSC", [P, 1])

        WH, WL = W[:, :, 0, :, :], W[:, :, 1, :, :]
        K_, V_, SO_ = (HEAD[:, HT * i:HT * (i + 1), :] for i in (0, 2, 3))
        VS = V_.rearrange("p (s a) b -> p s (a b)", s=ST)
        VB = HEAD[:, HT:HT + 2, :].rearrange("p a b -> p (a b)")
        KV_ = K_
        GW = HEAD[:, 2 * HT, :].rearrange("p (k g) -> p k g", k=KT)
        GS = YC[:, 0:KT // 2, :].rearrange("p k (a g) -> p (k a) g", a=2)
        GLOW, GATES = HEAD[0:NG, 2 * HT + 1, :], HEAD[0:NG, 2 * HT + 2, :]
        F_R, A_R, I_R, G_R, C_R, CB_R, Z_R, N_R = (HEAD[0:2 * H, i, :] for i in range(8))
        RS = EW[0:2 * H, 0:2, :]
        XROWS = M[:, :, :].rearrange("p (s a) b -> p s (a b)", s=ST)
        SQUARES = HEAD[:, :, :].rearrange("p (s a) b -> p s (a b)", s=ST)
        PROWS = CP[:, 0:(L * PBLK + 1) * P].rearrange("p (b c) -> p b c", c=P)

        ps = ctx.enter_context(nc.psum_tensor("ps", [P, 4, 2 * S], F32))
        px = ctx.enter_context(nc.psum_tensor("px", [P, 4, 2 * S], F32))

        x_rows_in = [sem(f"x_rows_in{i}") for i in range(2)]
        rows_in = sem("rows_in")
        bias_in = sem("bias_in")
        raw_in = [sem(f"raw_in{c}") for c in range(QC)]
        gate_in = sem("gate_in")
        hi_made = sem("hi_made")
        lo_made = sem("lo_made")
        multiplied = sem("multiplied")
        low_out = sem("low_out")
        pairs_out = sem("pairs_out")
        ident_made, ones_made, pads_made = sem("ident_made"), sem("ones_made"), sem("pads_made")
        rows_turned = sem("rows_turned")
        par_made = sem("par_made")
        x_turned = sem("x_turned")
        x_in = sem("x_in")
        x_summed = sem("x_summed")
        x_total = sem("x_total")
        squared = sem("squared")
        sq_added = sem("sq_added")
        summed = sem("summed")
        rms_made, inv_spread = sem("rms_made"), sem("inv_spread")
        h_made, h_hi, h_lo = sem("h_made"), sem("h_hi"), sem("h_lo")
        gw_hi, gw_lo = sem("gw_hi"), sem("gw_lo")
        gs_clear = sem("gs_clear")
        gates_mm, gates_low = sem("gates_mm"), sem("gates_low")
        gates_made, gates_turned = sem("gates_made"), sem("gates_turned")
        gcols_made, grows_mm = sem("gcols_made"), sem("grows_mm")
        f_abs, f_exp, f_log = sem("f_abs"), sem("f_exp"), sem("f_log")
        m_made, rows_made, ccol_mm = sem("m_made"), sem("rows_made"), sem("ccol_mm")
        glu_sig = sem("glu_sig")
        qk_summed, qk_silu = sem("qk_summed"), sem("qk_silu")
        rs_made = sem("rs_made")
        scores, m_spread, e_spread = sem("scores"), sem("m_spread"), sem("e_spread")
        e_ready, exp_made, masked = sem("e_ready"), sem("exp_made"), sem("masked")
        heads_seen = sem("heads_seen")
        pw_made, pw_summed = sem("pw_made"), sem("pw_summed")
        dens, dens_inv, dens_spread = sem("dens"), sem("dens_inv"), sem("dens_spread")
        a_made = sem("a_made")
        v_bias_in = sem("v_bias_in")
        v_made = sem("v_made")
        ht_mm, o_sig, ht_made = sem("ht_mm"), sem("o_sig"), sem("ht_made")
        ht_sq, ht_summed, ht_rms = sem("ht_sq"), sem("ht_summed"), sem("ht_rms")
        ht_added, ht_inv, ht_spread = sem("ht_added"), sem("ht_inv"), sem("ht_spread")
        z_silu, ya_made = sem("z_silu"), sem("ya_made")
        ya_hi, ya_lo = sem("ya_hi"), sem("ya_lo")
        ga_sig, gb_sig = sem("ga_sig"), sem("gb_sig")
        conv_made, mean_mm, centred = sem("conv_made"), sem("mean_mm"), sem("centred")
        c_sq, c_added = sem("c_sq"), sem("c_added")
        c_summed, ln_std = sem("c_summed"), sem("ln_std")
        zb_silu, ln_made, ln_silu = sem("zb_silu"), sem("ln_made"), sem("ln_silu")
        cb_made, cb_hi = sem("cb_made"), sem("cb_hi")
        cb_lo = sem("cb_lo")
        m_sum = sem("m_sum")
        m_hi, m_lo = sem("m_hi"), sem("m_lo")
        inv_made, y_turned = sem("inv_made"), sem("y_turned")
        y_vector, y_scalar = sem("y_vector"), sem("y_scalar")
        y_rows = [sem(f"y_rows{s}") for s in range(ST)]
        stored = sem("stored")
        dve_steps, pool_steps = sem("dve_steps"), sem("pool_steps")

        w_in_v = w_in.rearrange("l (k p) n -> l p k n", p=P)
        w_a_v, w_b_v, w_out_v = (w.rearrange("l (k p) n -> l p k n", p=P) for w in (w_a, w_b, w_out))
        out_v = out.rearrange("b (s p) d -> p (b s) d", p=P)

        row_loads = []

        def param_rows(row, src):
            n, done = src.shape[1], 0
            while done < n:
                at = row + done
                k = min(n - done, P - at % P)
                row_loads.append((PROWS[at % P:at % P + k, ds(at // P, L, PBLK), :],
                                  src[:, done:done + k, :].rearrange("l t c -> t l c")))
                done += k

        for column, vector in ((NORM_W, norm_w), (B_MAIN, b_in[:, 0:GATE0]),
                               (B_CONV, b_in[:, GATE0 + NG:]), (MNORM_W, mlstm_norm_w),
                               (DW_B, dw_b), (LN_W, ln_w), (LN_B, ln_b)):
            param_rows(column, vector.rearrange("l (t c) -> l t c", c=P))
        param_rows(QK_W, qk_conv_w.rearrange("l k (t c) -> l (k t) c", c=P))
        param_rows(DW_W, dw_w.rearrange("l k (t c) -> l (k t) c", c=P))
        row_loads.append((PROWS[0:KT, L * PBLK, :], final_norm_w.rearrange("(t c) -> t c", c=P)))

        def par(l, column, count=1, step=1):
            return PAR[:, ds(l * PARS + column, count, step)]

        def conv_in(tile, tap):
            return CP[:, ds(tile * CW + tap, S)]

        def conv_out(tile, count):
            return CP[:, tile * CW:(tile + count) * CW].rearrange(
                "p (t c) -> p t c", c=CW)[:, :, PAD:CW]

        def spread(rows, count):
            return rows.unsqueeze(1).to_broadcast([P, count, S])

        def buf(g):
            return (EW, QB)[g % 2]

        def duo_buf(p):
            return buf(p // 2)[:, 2 * (p % 2):2 * (p % 2) + 2, :]

        block = ctx.enter_context(nc.Block())

        @block.sync
        def _(sp):
            for i in range(2):
                cols = slice(i * D // 2, (i + 1) * D // 2)
                sp.dma_start(XROWS[:, :, cols], x.rearrange("b (s p) d -> p (b s) d", p=P)[:, :, cols]
                             ).then_inc(x_rows_in[i], 16)
            for dst, src in row_loads:
                sp.dma_start(dst, src).then_inc(rows_in, 16)
            sp.dma_start(GBIAS[:], b_in[:, GATE0:GATE0 + NG].rearrange("l g -> g l"),
                         allow_slow_non_contiguous=True).then_inc(bias_in, 16)

            def load_pair(w, l, col, n):
                for c in range(QC):
                    sp.wait_ge(lo_made, n * QC + (c + 1))
                    sp.dma_start(RAW[:, c, :, :], w[l, :, c * KQ:(c + 1) * KQ, ds(col, PC)]
                                 ).then_inc(raw_in[c], 16)

            with sp.Fori(0, L) as l:
                load_pair(w_in_v, l, GLU_A, sp.snap(l * NP))
                sp.wait_ge(cb_lo, l * H + 1)
                sp.dma_start(GW, w_in_v[l, :, :, GATE0:GATE0 + NG]).then_inc(gate_in, 16)
                load_pair(w_in_v, l, GLU_B, sp.snap(l * NP + 1))
                with sp.Fori(1, N_GLU // 2) as j:
                    n = sp.snap(l * NP + AT_GLU + j * 2)
                    load_pair(w_in_v, l, j * PC + GLU_A, n)
                    load_pair(w_in_v, l, j * PC + GLU_B, n + 1)
                with sp.Fori(0, H) as h:
                    n = sp.snap(l * NP + AT_HEAD + h * 10)
                    sp.wait_ge(v_made, l * H + h + 1)
                    sp.dma_start(VB, b_in[ds(l, 1), ds(h * DH + V_T * P, DH)].partition_broadcast(P)
                                 ).then_inc(v_bias_in, 16)
                    for i, first in enumerate((K_T, Q_T, V_T, O_T, Z_T)):
                        load_pair(w_in_v, l, h * DH + first * P, n + 2 * i)
                        load_pair(w_in_v, l, h * DH + (first * P + PC), n + (2 * i + 1))
                with sp.Fori(0, N_GA // 2) as j:
                    n = sp.snap(l * NP + AT_GA + j * 2)
                    load_pair(w_in_v, l, j * PC + G_A, n)
                    load_pair(w_a_v, l, j * PC, n + 1)
                with sp.Fori(0, N_ZB) as j:
                    load_pair(w_in_v, l, j * PC + Z_B, sp.snap(l * NP + AT_ZB + j))
                with sp.Fori(0, N_GB // 2) as j:
                    n = sp.snap(l * NP + AT_GB + j * 2)
                    load_pair(w_in_v, l, j * PC + G_B, n)
                    load_pair(w_b_v, l, j * PC, n + 1)
                with sp.Fori(0, N_OUT) as j:
                    load_pair(w_out_v, l, j * PC, sp.snap(l * NP + AT_OUT + j))
            for i in range(2):
                for s in range(ST):
                    sp.wait_ge(y_rows[s], i + 1)
                    cols = slice(i * D // 2, (i + 1) * D // 2)
                    sp.dma_start(out_v[:, s, cols], XROWS[:, s, cols]).then_inc(stored, 16)
            sp.wait_ge(stored, 2 * 16 * ST)

        @block.gpsimd
        def _(pool):
            steps = Steps(pool, pool_steps)
            steps.mark(nc.gpsimd.memset(IDENT[:], 0.0))
            steps.wait()
            nc.gpsimd.affine_select(out=IDENT[:], in_=IDENT[:], compare_op=ALU.not_equal, fill=1.0,
                                    base=0, pattern=[[-1, P]], channel_multiplier=1
                                    ).then_inc(ident_made, 1)
            nc.gpsimd.memset(YC[:, 0:KT // 2, :].bitcast(F32), 0.0).then_inc(gs_clear, 1)
            steps.mark(nc.gpsimd.memset(GC[:], 0.0))
            steps.mark(nc.gpsimd.memset(QPAD[:], 0.0))
            pool.wait_ge(rows_turned, 1)
            steps.mark(nc.gpsimd.memset(CP[:, 0:KT * CW].rearrange("p (t c) -> p t c", c=CW)
                                        [:, :, 0:PAD], 0.0))
            steps.mark(nc.gpsimd.memset(CP[:, KT * CW:], 0.0))
            steps.wait()
            pool.sem_inc(pads_made, 1)
            with pool.Fori(0, L) as l:
                n0 = pool.snap(l * NP)
                for c in range(QC):
                    pool.wait_ge(hi_made, n0 * QC + (c + 1))
                    nc.gpsimd.tensor_tensor(out=WL[:, c, :, :], in0=RAW[:, c, :, :],
                                            in1=WH[:, c, :, :].bitcast(F32), op=ALU.subtract
                                            ).then_inc(lo_made, 1)
                with pool.Fori(0, H) as h:
                    u = pool.snap(l * H + h)
                    pool.wait_ge(exp_made, u + 1)
                    pool.sem_inc(heads_seen, 1)
                    for d in range(2):
                        sign = 1 - 2 * d
                        w = EW[:, 2 * d:2 * d + 2, :]
                        nc.gpsimd.affine_select(out=w, in_=w, compare_op=ALU.is_ge, fill=0.0,
                                                base=0, pattern=[[-P * sign, ST], [sign, S]],
                                                channel_multiplier=-sign).then_inc(masked, 1)
                    pool.wait_ge(v_bias_in, u * 16 + 16)
                    pool.wait_ge(pairs_out, l * NP + h * 10 + (AT_HEAD + 8))
                    nc.gpsimd.tensor_tensor(out=VS, in0=VS,
                                            in1=VB.unsqueeze(1).to_broadcast([P, ST, DH]),
                                            op=ALU.add).then_inc(v_made, 1)

        @block.scalar
        def _(act):
            def split_hi(n, c):
                act.wait_ge(raw_in[c], n * 16 + 16)
                act.wait_ge(multiplied, n * QC + (c + 1))
                nc.scalar.copy(WH[:, c, :, :], RAW[:, c, :, :]).then_inc(hi_made, 1)

            def low_half(n, k, bias=None):
                act.wait_ge(multiplied, n * QC + (k + 2) * QC)
                act.wait_ge(pairs_out, n + (k + 1))
                q = k % 2
                if bias is None:
                    nc.scalar.copy(T[:, q, :, :], ps[:, 2 * q:2 * q + 2, S:2 * S]
                                   ).then_inc(low_out, 1)
                    return
                for t in range(2):
                    i = nc.scalar.activation(T[:, q, t, :], ps[:, 2 * q + t, S:2 * S], ACT.Identity,
                                             bias=bias(t))
                i.then_inc(low_out, 1)

            def split_rest(n, k, first=1, last=QC):
                for c in range(first, last):
                    split_hi(n + (k + 1), c)

            def split_and_low(n, k, bias=None):
                split_rest(n, k, 0)
                low_half(n, k, bias)

            def square_duo(l, d, tile, q):
                act.wait_ge(sq_added, l * (N_OUT - 1) + (d + 1))
                nc.scalar.activation(EW[:, 2 * q:2 * q + 2, :], X[:, ds(tile, 2), :], ACT.Square
                                     ).then_inc(squared, 1)

            def root(source, dst, done):
                nc.scalar.activation(dst, source, ACT.Sqrt, bias=EPSC[:], scale=1.0 / D
                                     ).then_inc(done, 1)

            for i in range(2):
                act.wait_ge(x_rows_in[i], 16)
                cols = slice(i * D // 2, (i + 1) * D // 2)
                for s in range(ST):
                    at = i * ST + s
                    nc.scalar.activation(SQUARES[:, s, cols], XROWS[:, s, cols], ACT.Square,
                                         accum_out=R4[:, at:at + 1]).then_inc(x_summed, 1)
            act.wait_ge(ones_made, 1)
            act.wait_ge(x_total, 1)
            root(R4[:, 0:ST], R4[:, 0:ST], rms_made)
            act.sem_inc(cb_lo, 1)
            act.sem_inc(v_made, 1)
            act.wait_ge(x_turned, 2)
            nc.scalar.copy(X[:, KT // 2:KT, :], px[:].rearrange("p a (b c) -> p (a b) c", c=S)
                           ).then_inc(x_in, 1)

            def sigmoid_out(n, k, where, done):
                act.wait_ge(pairs_out, n + (k + 3))
                nc.scalar.activation(where, where, ACT.Sigmoid).then_inc(done, 1)

            with act.Fori(0, L) as l:
                n0 = act.snap(l * NP)
                split_hi(n0, 0)
                for p in range(KT // 2):
                    act.wait_ge(h_made, l * (KT // 2) + (p + 1))
                    nc.scalar.copy(Hs[:, 2 * p:2 * p + 2, 0:S], duo_buf(p)).then_inc(h_hi, 1)
                    if p in (0, 2, 4):
                        split_hi(n0, p // 2 + 1)
                act.wait_ge(gate_in, l * 16 + 16)
                act.wait_ge(gs_clear, 1)
                nc.scalar.copy(GS[:, :, 0:NG], GW).then_inc(gw_hi, 1)

                def glu_bias(j, half):
                    return lambda t: par(l, j * 2 + (B_CONV + KT * half + t))

                split_and_low(n0, 0, glu_bias(0, 0))
                split_rest(n0, 1, 0, 1)
                act.wait_ge(bias_in, 16)
                act.wait_ge(gates_mm, l + 1)
                nc.scalar.activation(GLOW, px[0:NG, 0, S:2 * S], ACT.Identity,
                                     bias=GBIAS[:, ds(l, 1)]).then_inc(gates_low, 1)
                split_rest(n0, 1)
                low_half(n0, 1, glu_bias(0, 1))
                sigmoid_out(n0, 1, QB[:, 2:4, :], glu_sig)
                split_rest(n0, 2, 0, 1)
                act.wait_ge(grows_mm, l + 1)
                nc.scalar.activation(A_R, px[0:2 * H, 2, S:2 * S], ACT.Abs)
                nc.scalar.copy(I_R, px[0:2 * H, 2, 0:S]).then_inc(f_abs, 1)
                act.wait_ge(f_abs, l + 1)
                nc.scalar.activation(A_R, A_R, ACT.Exp, scale=-1.0).then_inc(f_exp, 1)
                act.wait_ge(f_exp, l + 1)
                nc.scalar.activation(A_R, A_R, ACT.Ln, bias=1.0).then_inc(f_log, 1)
                split_rest(n0, 2)
                low_half(n0, 2, glu_bias(1, 0))
                split_rest(n0, 3, 0, 1)
                act.wait_ge(m_made, l + 1)
                nc.scalar.activation(ROWS[:, 1, :], ROWS[:, 1, :], ACT.Exp)
                nc.scalar.activation(N_R, N_R, ACT.Exp).then_inc(rows_made, 1)
                split_rest(n0, 3)
                low_half(n0, 3, glu_bias(1, 1))
                sigmoid_out(n0, 3, QB[:, 2:4, :], glu_sig)
                with act.Fori(2, N_GLU // 2) as j:
                    n = act.snap(l * NP + j * 2)
                    split_and_low(n, 0, glu_bias(j, 0))
                    split_and_low(n, 1, glu_bias(j, 1))
                    sigmoid_out(n, 1, QB[:, 2:4, :], glu_sig)

                split_hi(l * NP + (AT_HEAD + 1), 0)
                with act.Fori(0, H) as h:
                    n = act.snap(l * NP + AT_HEAD + h * 10)
                    u = act.snap(l * H + h)

                    def bias(first):
                        return lambda t: par(l, h * HT + (B_MAIN + first + t))

                    split_rest(n, 0)
                    low_half(n, 0, bias(K_T))
                    for i, first in enumerate((K_T + 2, Q_T, Q_T + 2, None)):
                        split_rest(n, i + 1, 0, 1)
                        if i == 0:
                            act.wait_ge(e_ready, u + 1)
                            nc.scalar.activation(EW[:], EW[:], ACT.Exp, scale=-1.0
                                                 ).then_inc(exp_made, 1)
                        act.wait_ge(qk_summed, u * 4 + (i + 1))
                        b = (K_, QB)[i // 2][:, 2 * (i % 2):2 * (i % 2) + 2, :]
                        nc.scalar.activation(b, b, ACT.Silu).then_inc(qk_silu, 1)
                        split_rest(n, i + 1)
                        low_half(n, i + 1, None if first is None else bias(first))
                    split_and_low(n, 5)
                    split_and_low(n, 6, bias(O_T))
                    split_rest(n, 7, 0, 1)
                    sigmoid_out(n, 6, SO_[:, 0:2, :], o_sig)
                    split_rest(n, 7)
                    low_half(n, 7, bias(O_T + 2))
                    sigmoid_out(n, 7, SO_[:, 2:4, :], o_sig)
                    split_rest(n, 8, 0, 2)
                    act.wait_ge(ht_made, u + 1)
                    nc.scalar.activation(EW[:], KV_, ACT.Square).then_inc(ht_sq, 1)
                    split_rest(n, 8, 2)
                    low_half(n, 8, bias(Z_T))
                    split_rest(n, 9, 0, 1)
                    act.wait_ge(ht_summed, u + 1)
                    nc.scalar.activation(R4[:, 0:ST], px[:, 0:ST, 0], ACT.Sqrt, bias=EPSC[:],
                                         scale=1.0 / DH).then_inc(ht_rms, 1)
                    split_rest(n, 9, 1, 2)
                    for i in range(2):
                        if i == 1:
                            split_rest(n, 9, 2)
                            low_half(n, 9, bias(Z_T + 2))
                        act.wait_ge(pairs_out, n + (i + 11))
                        z = QB[:, 2 * i:2 * i + 2, :]
                        nc.scalar.activation(z, z, ACT.Silu).then_inc(z_silu, 1)
                    split_hi(n + 11, 0)
                    act.wait_ge(ya_made, u + 1)
                    nc.scalar.copy(YC[:, ds(h * HT, HT), 0:S], KV_).then_inc(ya_hi, 1)

                with act.Fori(0, N_GA // 2) as j:
                    n = act.snap(l * NP + AT_GA + j * 2)
                    split_rest(n, 0)
                    low_half(n, 0, lambda t: par(l, j * 2 + (B_CONV + 3 * KT + t)))
                    sigmoid_out(n, 0, QB[:, 0:2, :], ga_sig)
                    split_and_low(n, 1)
                    split_hi(n + 3, 0)

                n = act.snap(l * NP + AT_ZB)

                def zb_bias(j):
                    return lambda t: par(l, B_CONV + 2 * KT + 2 * j + t)

                def silu_zb(j):
                    act.wait_ge(pairs_out, n + (j + 3))
                    z = HEAD[:, 2 * j:2 * j + 2, :]
                    nc.scalar.activation(z, z, ACT.Silu).then_inc(zb_silu, 1)

                def square_c(g):
                    if g >= 2:
                        act.wait_ge(c_added, l * 4 + (g - 1))
                    act.wait_ge(centred, l * 4 + (g + 1))
                    nc.scalar.activation(buf(min(g, 1))[:], conv_out(4 * g, 4), ACT.Square
                                         ).then_inc(c_sq, 1)

                def ln_act(g):
                    act.wait_ge(ln_made, l * 4 + (g + 1))
                    for t in range(4):
                        b = buf(g)[:, t, :]
                        i = nc.scalar.activation(b, b, ACT.Silu, scale=par(l, LN_W + 4 * g + t),
                                                 bias=par(l, LN_B + 4 * g + t))
                    i.then_inc(ln_silu, 1)

                def cb_high(g):
                    act.wait_ge(cb_made, l * 4 + (g + 1))
                    nc.scalar.copy(YC[:, 4 * g:4 * g + 4, 0:S], buf(g)[:]).then_inc(cb_hi, 1)

                split_rest(n, 0)
                low_half(n, 0, zb_bias(0))
                split_rest(n, 1, 0, 3)
                square_c(0)
                square_c(1)
                split_rest(n, 1, 3)
                low_half(n, 1, zb_bias(1))
                square_c(2)
                split_rest(n, 2, 0, 1)
                square_c(3)
                split_rest(n, 2)
                low_half(n, 2, zb_bias(2))
                split_rest(n, 3, 0, 1)
                act.wait_ge(c_summed, l + 1)
                nc.scalar.activation(RR[:], px[:, 1, 0:S], ACT.Sqrt, bias=EPSC[:], scale=1.0 / D
                                     ).then_inc(ln_std, 1)
                split_rest(n, 3)
                low_half(n, 3, zb_bias(3))
                for j in range(4):
                    silu_zb(j)
                for g in range(3):
                    split_rest(n, g + 4, 0, 1)
                    ln_act(g)
                    split_rest(n, g + 4, 1, 3)
                    cb_high(g)
                    split_rest(n, g + 4, 3)
                    low_half(n, g + 4, zb_bias(g + 4))
                    silu_zb(g + 4)
                split_rest(n, 7, 0, 1)
                ln_act(3)
                split_rest(n, 7)
                low_half(n, 7, zb_bias(7))
                silu_zb(7)
                split_hi(n + 9, 0)
                cb_high(3)

                def g_b(j, n):
                    split_rest(n, 0)
                    low_half(n, 0, lambda t: par(l, j * 2 + (B_CONV + 4 * KT + t)))
                    sigmoid_out(n, 0, QB[:, 0:2, :], gb_sig)

                with act.Fori(0, N_GB // 2 - 1) as j:
                    n = act.snap(l * NP + AT_GB + j * 2)
                    g_b(j, n)
                    split_and_low(n, 1)
                    split_hi(n + 3, 0)
                n = act.snap(l * NP + (AT_OUT - 2))
                g_b(N_GB // 2 - 1, n)
                act.wait_ge(multiplied, n * QC + 2 * QC)
                for g in range(3):
                    act.wait_ge(m_sum, l * (N_GB // 2) + (2 * g + 3))
                    nc.scalar.copy(Hs[:, 4 * g:4 * g + 4, 0:S], M[:, 4 * g:4 * g + 4, :]
                                   ).then_inc(m_hi, 1)
                    split_hi(n + 2, g)
                low_half(n, 1)
                act.wait_ge(m_sum, l * (N_GB // 2) + (N_GB // 2 + 1))
                nc.scalar.copy(Hs[:, 12:16, 0:S], M[:, 12:16, :]).then_inc(m_hi, 1)
                split_hi(n + 2, 3)

                def out_duo(n, k, d):
                    split_rest(n, k, 0)
                    act.wait_ge(pairs_out, n + (k + 3))
                    square_duo(l, d, d * 2, k)

                with act.Fori(0, N_OUT // 2 - 1) as j:
                    n = act.snap(l * NP + AT_OUT + j * 2)
                    out_duo(n, 0, j * 2)
                    out_duo(n, 1, j * 2 + 1)
                n = act.snap(l * NP + (NP - 2))
                out_duo(n, 0, N_OUT - 2)
                nc.scalar.activation(R4[:, 2:3], EPSC[:], ACT.Sqrt)
                act.wait_ge(pairs_out, n + 4)
                square_duo(l, N_OUT - 1, KT - 2, 1)
                act.wait_ge(summed, l + 1)
                root(px[:, 0:ST, 0], R4[:, 0:ST], rms_made)

            for t in range(Y_SPLIT, KT):
                nc.scalar.activation(HEAD[:, t, :], X[:, t, :], ACT.Identity,
                                     scale=PAR[:, L * PARS + t:L * PARS + t + 1]
                                     ).then_inc(y_scalar, 1)
            act.wait_ge(inv_made, L + 1)
            for i in range(2):
                act.wait_ge(y_turned, 2 * i + 2)
                cols = slice(i * D // 2, (i + 1) * D // 2)
                nc.scalar.activation(XROWS[:, 1, cols], ps[:].rearrange("p a b -> p (a b)")[:, cols],
                                     ACT.Identity, scale=R4[:, 1:2]).then_inc(y_rows[1], 1)
        @block.vector
        def _(dve):
            steps = Steps(dve, dve_steps)
            v = nc.vector

            def split_lo(n, c):
                dve.wait_ge(hi_made, n * QC + (c + 1))
                v.tensor_tensor(WL[:, c, :, :], RAW[:, c, :, :], WH[:, c, :, :].bitcast(F32),
                                ALU.subtract).then_inc(lo_made, 1)

            def pair_out(n, k, dst):
                dve.wait_ge(low_out, n + (k + 1))
                q = k % 2
                v.tensor_tensor(dst, ps[:, 2 * q:2 * q + 2, 0:S], T[:, q, :, :], ALU.add
                                ).then_inc(pairs_out, 1)

            def split_next(n, k):
                for c in range(QC):
                    split_lo(n + (k + 1), c)

            v.memset(EPSC[:], EPS)
            v.memset(ONES[:], 1.0).then_inc(ones_made, 1)
            dve.sem_inc(lo_made, QC)
            dve.sem_inc(sq_added, 2)
            dve.sem_inc(m_sum, 1)
            dve.wait_ge(x_turned, 1)
            steps.mark(v.tensor_copy(X[:, 0:KT // 2, :],
                                     ps[:].rearrange("p a (b c) -> p (a b) c", c=S)))
            steps.wait()
            dve.sem_inc(pairs_out, 2)
            dve.wait_ge(x_summed, 2 * ST)
            v.tensor_tensor(R4[:, 0:ST], R4[:, 0:ST], R4[:, ST:2 * ST], ALU.add).then_inc(x_total, 1)
            dve.wait_ge(rows_turned, 1)
            v.tensor_copy(PAR[:], ps[:].rearrange("p a b -> p (a b)")[:, 0:L * PARS + KT]
                          ).then_inc(par_made, 1)
            dve.wait_ge(par_made, 1)
            dve.wait_ge(x_in, 1)

            def add_squares(l, d, q):
                dve.wait_ge(squared, l * N_OUT + (d + 1))
                dve.wait_ge(sq_added, l * (N_OUT - 1) + (d + 2))
                v.tensor_tensor(ACC[:], ACC[:], EW[:, 2 * q:2 * q + 2, :], ALU.add
                                ).then_inc(sq_added, 1)

            def inverse_rms(l):
                dve.wait_ge(rms_made, l + 1)
                v.reciprocal(R4[:, 0:ST], R4[:, 0:ST]).then_inc(inv_made, 1)

            def scale_x(tile, weight, dst):
                return v.scalar_tensor_tensor(out=dst, in0=X[:, tile, :], scalar=weight,
                                              in1=px[:, 0, S:2 * S], op0=ALU.mult, op1=ALU.mult)

            with dve.Fori(0, L) as l:
                steps.enter(l, LAYER_STEPS)
                n0 = dve.snap(l * NP)

                def norm_duo(p):
                    if p >= 4:
                        dve.wait_ge(h_lo, l * (KT // 2) + (p - 3))
                    for t in range(2):
                        i = scale_x(2 * p + t, par(l, NORM_W + 2 * p + t), duo_buf(p)[:, t, :])
                    i.then_inc(h_made, 1)

                def duo_low(p):
                    dve.wait_ge(h_hi, l * (KT // 2) + (p + 1))
                    v.tensor_tensor(Hs[:, 2 * p:2 * p + 2, S:2 * S], duo_buf(p),
                                    Hs[:, 2 * p:2 * p + 2, 0:S].bitcast(F32), ALU.subtract
                                    ).then_inc(h_lo, 1)

                inverse_rms(l)
                dve.wait_ge(inv_spread, l + 1)
                norm_duo(0)
                for p in range(KT // 2):
                    if p + 1 < KT // 2:
                        norm_duo(p + 1)
                    duo_low(p)
                dve.wait_ge(gate_in, l * 16 + 16)
                dve.wait_ge(gw_hi, l + 1)
                v.tensor_tensor(GS[:, :, P:P + NG], GW, GS[:, :, 0:NG].bitcast(F32), ALU.subtract
                                ).then_inc(gw_lo, 1)

                taps = [k for k in range(DW_TAPS) if k != PAD] + [PAD]

                def conv_begin(tile):
                    steps.wait()
                    for t in range(2):
                        steps.mark(v.tensor_copy(CWT[:, t, 0:DW_TAPS],
                                                 par(l, tile + (DW_W + t), DW_TAPS, KT)))
                        steps.mark(v.tensor_copy(CWT[:, t, DW_TAPS:DW_TAPS + 1],
                                                 par(l, tile + (DW_B + t))))

                def conv_taps(tile, first, last):
                    for i in range(first, last):
                        k = taps[i]
                        for t in range(2):
                            steps.wait(1)
                            src, w = conv_in(tile + t, k), CWT[:, t, k:k + 1]
                            if i == 0:
                                steps.mark(v.tensor_scalar(ACC[:, t, :], src, w,
                                                           CWT[:, t, DW_TAPS:DW_TAPS + 1],
                                                           ALU.mult, ALU.add))
                            else:
                                dst = src if k == PAD else ACC[:, t, :]
                                steps.mark(v.scalar_tensor_tensor(
                                    out=dst, in0=src, scalar=w, in1=ACC[:, t, :],
                                    op0=ALU.mult, op1=ALU.add))

                def glu_mul(tile, unit):
                    dve.wait_ge(glu_sig, unit)
                    dst = CP[:, ds(tile * CW, 2 * CW)].rearrange("p (t c) -> p t c", c=CW)
                    steps.mark(v.tensor_tensor(dst[:, :, PAD:CW], QB[:, 0:2, :], QB[:, 2:4, :],
                                               ALU.mult))

                dve.wait_ge(lo_made, n0 * QC + 2 * QC)
                split_next(n0, 0)
                pair_out(n0, 0, QB[:, 0:2, :])
                split_lo(n0 + 2, 0)
                dve.wait_ge(gates_low, l + 1)
                v.tensor_tensor(GATES, px[0:NG, 0, 0:S], GLOW, ALU.add).then_inc(gates_made, 1)
                split_lo(n0 + 2, 1)
                split_lo(n0 + 2, 2)
                dve.wait_ge(pads_made, 1)
                dve.wait_ge(gates_turned, l + 1)
                for group, (kind, row) in enumerate(((0, 0), (2, 0), (1, H), (3, H))):
                    i = v.tensor_copy(GC[:, :, kind, row:row + H],
                                      px[:, 0:ST, H * group:H * group + H])
                i.then_inc(gcols_made, 1)
                split_lo(n0 + 2, 3)
                pair_out(n0, 1, QB[:, 2:4, :])
                glu_mul(0, l * (N_GLU // 2) + 1)
                split_lo(n0 + 3, 0)
                dve.wait_ge(f_abs, l + 1)
                steps.mark(v.tensor_scalar(F_R, px[0:2 * H, 2, S:2 * S], 0.0, None, ALU.min))
                steps.mark(v.memset(Z_R, 0.0))
                steps.wait()
                dve.wait_ge(f_log, l + 1)
                steps.mark(v.tensor_tensor(F_R, F_R, A_R, ALU.subtract))
                steps.wait()
                steps.mark(v.tensor_tensor_scan(G_R, F_R, Z_R, 0.0, ALU.add, ALU.add))
                steps.wait()
                steps.mark(v.tensor_tensor(C_R, I_R, G_R, ALU.subtract))
                steps.wait()
                steps.mark(v.tensor_tensor_scan(ROWS[:, 0, :], C_R, C_R, 0.0, ALU.max, ALU.max))
                steps.mark(v.tensor_copy(CB_R, C_R[:, ::-1]))
                steps.wait(1)
                steps.mark(v.scalar_tensor_tensor(out=N_R, in0=G_R, scalar=-1.0, in1=ROWS[:, 0, :],
                                                  op0=ALU.mult, op1=ALU.subtract))
                steps.wait()
                steps.mark(v.tensor_scalar(N_R, N_R, EXP_CAP, None, ALU.min))
                steps.wait()
                v.tensor_copy(ROWS[:, 1, :], N_R[:, ::-1]).then_inc(m_made, 1)
                for c in range(1, QC):
                    split_lo(n0 + 3, c)
                pair_out(n0, 2, QB[:, 0:2, :])
                split_next(n0, 3)
                pair_out(n0, 3, QB[:, 2:4, :])
                dve.wait_ge(ccol_mm, l + 1)
                cc = px[:, 3, 0:4 * ST * H].rearrange("p (s c) -> p s c", s=ST)
                steps.mark(v.tensor_copy(CCOL[:, :, 0:H], cc[:, :, 0:H]))
                steps.mark(v.tensor_copy(CCOL[:, :, H:2 * H], cc[:, :, 3 * H:4 * H]))
                ec = px[:, 3, 4 * ST * H:8 * ST * H].rearrange("p (s c) -> p s c", s=ST)
                for d in range(2):
                    steps.mark(v.tensor_copy(
                        ECOL[:, d, :, :].rearrange("p h s -> p s h"),
                        ec[:, :, 3 * d * H:(3 * d + 1) * H]))
                glu_mul(2, l * (N_GLU // 2) + 2)

                with dve.Fori(0, 2) as i:
                    steps.enter(i, 3 + 4 + 2 * DW_TAPS)
                    n = dve.snap(l * NP + 4 + i * 6)
                    duo = dve.snap(i * 2)
                    conv_begin(duo)
                    for j in range(3):
                        for k, dst, first, last in ((2 * j, QB[:, 0:2, :], 10 * j, 10 * j + 5),
                                                    (2 * j + 1, QB[:, 2:4, :], 10 * j + 5,
                                                     10 * j + 10 + j // 2)):
                            split_lo(n + (k + 1), 0)
                            conv_taps(duo, first, first + 2)
                            split_lo(n + (k + 1), 1)
                            conv_taps(duo, first + 2, first + 4)
                            split_lo(n + (k + 1), 2)
                            conv_taps(duo, first + 4, last)
                            split_lo(n + (k + 1), 3)
                            pair_out(n, k, dst)
                        glu_mul(i * 6 + (4 + 2 * j), l * (N_GLU // 2) + i * 3 + (3 + j))
                    steps.leave(2)

                split_lo(l * NP + (AT_HEAD + 1), 0)
                with dve.Fori(0, H) as h:
                    steps.enter(h, HEAD_STEPS)
                    n = dve.snap(l * NP + AT_HEAD + h * 10)
                    u = dve.snap(l * H + h)
                    duo = dve.snap(h * 2 + 4)

                    def with_taps(k, a, b, first=0):
                        cut = [a + (b - a) * max(c - first, 0) // (3 - first) for c in range(4)]
                        for c in range(first, QC):
                            split_lo(n + (k + 1), c)
                            if c < 3:
                                conv_taps(duo, cut[c], cut[c + 1])

                    def narrow_conv(i, dst, first):
                        dve.wait_ge(pairs_out, n + (i + 3))
                        for tap in range(QK_TAPS):
                            for t in range(2):
                                src = QPAD[:, t, tap:tap + S]
                                w = par(l, h * HT + (QK_W + tap * 2 * KT + first + t))
                                if tap == 0:
                                    steps.mark(v.tensor_scalar(dst[:, t, :], src, w, None, ALU.mult))
                                    continue
                                steps.wait(1)
                                ins = v.scalar_tensor_tensor(out=dst[:, t, :], in0=src, scalar=w,
                                                             in1=dst[:, t, :], op0=ALU.mult,
                                                             op1=ALU.add)
                                if tap == QK_TAPS - 1 and t == 1:
                                    ins.then_inc(qk_summed, 1)
                                else:
                                    steps.mark(ins)

                    def one_head_rows():
                        v.tensor_scalar(RS[:, 0, :], ROWS[:, 0, :], IDENT[0:2 * H, ds(h, 1)],
                                        None, ALU.mult)
                        v.tensor_scalar(RS[:, 1, :], ROWS[:, 0, ::-1],
                                        IDENT[0:2 * H, ds(h + H, 1)], None, ALU.mult
                                        ).then_inc(rs_made, 1)

                    conv_begin(duo)
                    one_head_rows()
                    with_taps(0, 0, 1, 1)
                    pair_out(n, 0, QPAD[:, :, 2:2 + S])
                    dve.wait_ge(m_spread, u + 1)
                    for d in range(2):
                        for st in range(ST):
                            i = v.tensor_scalar(EW[:, 2 * d + st, :], px[:, 1, d * S:(d + 1) * S],
                                                CCOL[:, st, ds(h + d * H, 1)], 0.0,
                                                ALU.subtract, ALU.max)
                    i.then_inc(e_ready, 1)
                    narrow_conv(0, K_[:, 0:2, :], KT)
                    with_taps(1, 1, 1)
                    dve.wait_ge(qk_summed, u * 4 + 1)
                    pair_out(n, 1, QPAD[:, :, 2:2 + S])
                    narrow_conv(1, K_[:, 2:4, :], KT + 2)
                    with_taps(2, 1, 2)
                    dve.wait_ge(qk_summed, u * 4 + 2)
                    pair_out(n, 2, QPAD[:, :, 2:2 + S])
                    narrow_conv(2, QB[:, 0:2, :], 0)
                    with_taps(3, 2, 3)
                    dve.wait_ge(qk_summed, u * 4 + 3)
                    pair_out(n, 3, QPAD[:, :, 2:2 + S])
                    narrow_conv(3, QB[:, 2:4, :], 2)
                    with_taps(4, 3, 9)
                    pair_out(n, 4, VS[:, :, 0:PC])
                    split_lo(n + 6, 0)
                    dve.wait_ge(scores, u + 1)
                    sc = px[:, 0, :].rearrange("p (a b) -> p a b", a=ST)
                    for d in range(2):
                        dve.wait_ge(masked, u * 2 + (d + 1))
                        i = v.scalar_tensor_tensor(out=QB[:, 2 * d:2 * d + 2, :], in0=sc,
                                                   scalar=float(DH) ** -0.5,
                                                   in1=EW[:, 2 * d:2 * d + 2, :],
                                                   op0=ALU.mult, op1=ALU.mult)
                    i.then_inc(pw_made, 1)
                    dve.wait_ge(pw_made, u + 1)
                    v.tensor_tensor(EW[:, 0:2, :], QB[:, 0:4:2, :], QB[:, 1:4:2, :], ALU.add
                                    ).then_inc(pw_summed, 1)
                    conv_taps(duo, 9, 11)
                    split_lo(n + 6, 1)
                    conv_taps(duo, 11, 13)
                    split_lo(n + 6, 2)
                    conv_taps(duo, 13, 15)
                    split_lo(n + 6, 3)
                    pair_out(n, 5, VS[:, :, PC:2 * PC])
                    split_lo(n + 7, 0)
                    dve.wait_ge(dens, u + 1)
                    r4, den = (x.rearrange("p (d a s) -> p d a s", d=2, a=1)
                               for x in (R4, px[:, 1, 0:2 * ST]))
                    steps.mark(v.scalar_tensor_tensor(out=r4, in0=den, scalar=-1.0,
                                                      in1=ECOL[:, :, ds(h, 1), :],
                                                      op0=ALU.mult, op1=ALU.max))
                    steps.wait()
                    steps.mark(v.tensor_tensor(R4, R4, px[:, 1, 0:2 * ST], ALU.max))
                    steps.wait()
                    v.reciprocal(R4, R4).then_inc(dens_inv, 1)
                    split_lo(n + 7, 1)
                    conv_taps(duo, 15, 18)
                    split_lo(n + 7, 2)
                    conv_taps(duo, 18, 20)
                    split_lo(n + 7, 3)
                    pair_out(n, 6, SO_[:, 0:2, :])
                    split_lo(n + 8, 0)
                    dve.wait_ge(dens_spread, u + 1)
                    for d in range(2):
                        q = QB[:, 2 * d:2 * d + 2, :]
                        steps.mark(v.tensor_tensor(q, q, spread(px[:, 0, d * S:(d + 1) * S], 2),
                                                   ALU.mult))
                    steps.wait()
                    v.tensor_tensor(QB[:, 0:2, :], QB[:, 0:2, :], QB[:, 2:4, :], ALU.add
                                    ).then_inc(a_made, 1)
                    with_taps(7, 20, 24, 1)
                    pair_out(n, 7, SO_[:, 2:4, :])
                    split_lo(n + 9, 0)
                    dve.wait_ge(ht_mm, u + 1)
                    dve.wait_ge(o_sig, u * 2 + 2)
                    v.tensor_tensor(KV_, px[:, 2:4, :].rearrange("p a (b c) -> p (a b) c", c=S), SO_,
                                    ALU.mult).then_inc(ht_made, 1)
                    split_lo(n + 9, 1)
                    conv_taps(duo, 24, 26)
                    dve.wait_ge(ht_sq, u + 1)
                    steps.mark(v.tensor_tensor(EW[:, 0:2, :], EW[:, 0:2, :], EW[:, 2:4, :], ALU.add))
                    steps.wait()
                    v.tensor_tensor(EW[:, 0, :], EW[:, 0, :], EW[:, 1, :], ALU.add
                                    ).then_inc(ht_added, 1)
                    split_lo(n + 9, 2)
                    conv_taps(duo, 26, 29)
                    split_lo(n + 9, 3)
                    pair_out(n, 8, QB[:, 0:2, :])
                    dve.wait_ge(ht_rms, u + 1)
                    v.reciprocal(R4[:, 0:ST], R4[:, 0:ST]).then_inc(ht_inv, 1)
                    split_lo(n + 10, 0)
                    conv_taps(duo, 29, DW_TAPS)
                    split_lo(n + 10, 1)
                    dve.wait_ge(ht_spread, u + 1)
                    steps.mark(v.tensor_tensor(KV_, KV_, spread(px[:, 0, S:2 * S], HT), ALU.mult))
                    split_lo(n + 10, 2)
                    split_lo(n + 10, 3)
                    pair_out(n, 9, QB[:, 2:4, :])
                    steps.wait()
                    for t in range(HT):
                        if t % 2 == 0:
                            dve.wait_ge(z_silu, u * 2 + (t // 2 + 1))
                        i = v.scalar_tensor_tensor(out=KV_[:, t, :], in0=KV_[:, t, :],
                                                   scalar=par(l, h * HT + (MNORM_W + t)),
                                                   in1=QB[:, t, :], op0=ALU.mult, op1=ALU.mult)
                    i.then_inc(ya_made, 1)
                    split_lo(n + 11, 0)
                    dve.wait_ge(ya_hi, u + 1)
                    v.tensor_tensor(YC[:, ds(h * HT, HT), S:2 * S], KV_,
                                    YC[:, ds(h * HT, HT), 0:S].bitcast(F32), ALU.subtract
                                    ).then_inc(ya_lo, 1)
                    steps.leave(H)

                with dve.Fori(0, 2) as i:
                    steps.enter(i, 4 + 4 + 2 * DW_TAPS)
                    n = dve.snap(l * NP + AT_GA + i * 8)
                    duo = dve.snap(i * 2 + 12)
                    conv_begin(duo)
                    for j in range(4):
                        for k, dst in ((2 * j, QB[:, 0:2, :]), (2 * j + 1, QB[:, 2:4, :])):
                            if k % 2 == 1:
                                split_lo(n + (k + 1), 0)
                            split_lo(n + (k + 1), 1)
                            conv_taps(duo, 4 * k, 4 * k + 2)
                            split_lo(n + (k + 1), 2)
                            conv_taps(duo, 4 * k + 2, min(4 * k + 4, DW_TAPS))
                            split_lo(n + (k + 1), 3)
                            pair_out(n, k, dst)
                        split_lo(n + (2 * j + 3), 0)
                        dve.wait_ge(pairs_out, n + (2 * j + 4))
                        dve.wait_ge(ga_sig, l * (N_GA // 2) + i * 4 + (j + 1))
                        steps.mark(v.tensor_tensor(M[:, ds(i * 8 + 2 * j, 2), :], QB[:, 0:2, :],
                                                   QB[:, 2:4, :], ALU.mult))
                    steps.leave(2)
                n = dve.snap(l * NP + AT_ZB)

                def scale_c(g):
                    v.tensor_tensor(buf(g)[:], conv_out(4 * g, 4), spread(RR[:], 4), ALU.mult
                                    ).then_inc(ln_made, 1)

                def gate_c(g):
                    dve.wait_ge(ln_silu, l * 4 + (g + 1))
                    dve.wait_ge(zb_silu, l * N_ZB + (2 * g + 2))
                    v.tensor_tensor(buf(g)[:], buf(g)[:], HEAD[:, 4 * g:4 * g + 4, :], ALU.mult
                                    ).then_inc(cb_made, 1)

                def low_c(g):
                    dve.wait_ge(cb_hi, l * 4 + (g + 1))
                    v.tensor_tensor(YC[:, 4 * g:4 * g + 4, S:2 * S], buf(g)[:],
                                    YC[:, 4 * g:4 * g + 4, 0:S].bitcast(F32), ALU.subtract
                                    ).then_inc(cb_lo, 1)

                for g in range(1, 4):
                    steps.wait()
                    steps.mark(v.tensor_tensor(EW[:], conv_out(0, 4) if g == 1 else EW[:],
                                               conv_out(4 * g, 4), ALU.add))
                steps.wait()
                v.tensor_tensor(EW[:, 0:2, :], EW[:, 0:2, :], EW[:, 2:4, :], ALU.add
                                ).then_inc(conv_made, 1)
                for c in range(1, QC):
                    split_lo(n + 1, c)
                pair_out(n, 0, HEAD[:, 0:2, :])
                split_lo(n + 2, 0)
                dve.wait_ge(mean_mm, l + 1)
                steps.mark(v.tensor_scalar(RR[:], px[:, 0, 0:S], 1.0 / D, None, ALU.mult))
                steps.wait()
                for g in range(4):
                    v.tensor_tensor(conv_out(4 * g, 4), conv_out(4 * g, 4), spread(RR[:], 4),
                                    ALU.subtract).then_inc(centred, 1)
                    if g < 2:
                        split_lo(n + 2, g + 1)

                def add_c(g):
                    dve.wait_ge(c_sq, l * 4 + (g + 1))
                    if g > 1:
                        dve.wait_ge(c_added, l * 4 + (g - 1))
                    v.tensor_tensor(EW[:], EW[:], QB[:], ALU.add).then_inc(c_added, 1)

                add_c(1)
                split_lo(n + 2, 3)
                pair_out(n, 1, HEAD[:, 2:4, :])
                add_c(2)
                split_lo(n + 3, 0)
                add_c(3)
                dve.wait_ge(c_added, l * 4 + 3)
                v.tensor_tensor(EW[:, 0:2, :], EW[:, 0:2, :], EW[:, 2:4, :], ALU.add
                                ).then_inc(c_added, 1)
                for c in range(1, QC):
                    split_lo(n + 3, c)
                pair_out(n, 2, HEAD[:, 4:6, :])
                split_lo(n + 4, 0)
                dve.wait_ge(ln_std, l + 1)
                steps.mark(v.reciprocal(RR[:], RR[:]))
                split_lo(n + 4, 1)
                steps.wait()
                scale_c(0)
                split_lo(n + 4, 2)
                split_lo(n + 4, 3)
                pair_out(n, 3, HEAD[:, 6:8, :])
                for g in range(3):
                    split_lo(n + (g + 5), 0)
                    gate_c(g)
                    split_lo(n + (g + 5), 1)
                    if g > 0:
                        dve.wait_ge(cb_lo, l * 4 + (g + 1))
                    scale_c(g + 1)
                    split_lo(n + (g + 5), 2)
                    dve.wait_ge(cb_made, l * 4 + (g + 1))
                    low_c(g)
                    split_lo(n + (g + 5), 3)
                    pair_out(n, g + 4, HEAD[:, 2 * g + 8:2 * g + 10, :])
                split_next(n, 7)
                pair_out(n, 7, HEAD[:, 14:16, :])
                gate_c(3)
                split_lo(n + 9, 0)
                dve.wait_ge(cb_made, l * 4 + 4)
                low_c(3)

                def add_b(tile, unit, n, k):
                    dve.wait_ge(pairs_out, n + (k + 3))
                    dve.wait_ge(gb_sig, unit)
                    steps.mark(v.tensor_tensor(QB[:, 2:4, :], QB[:, 0:2, :], QB[:, 2:4, :],
                                               ALU.mult))
                    steps.wait()
                    m = M[:, ds(tile, 2), :]
                    v.tensor_tensor(m, m, QB[:, 2:4, :], ALU.add).then_inc(m_sum, 1)

                with dve.Fori(0, N_GB // 2 - 1) as j:
                    steps.enter(j, 1)
                    n = dve.snap(l * NP + AT_GB + j * 2)
                    for c in range(1, QC):
                        split_lo(n + 1, c)
                    dve.wait_ge(cb_lo, l * 4 + 5)
                    dve.wait_ge(m_sum, l * (N_GB // 2) + j + 1)
                    pair_out(n, 0, QB[:, 0:2, :])
                    split_next(n, 1)
                    pair_out(n, 1, QB[:, 2:4, :])
                    split_lo(n + 3, 0)
                    add_b(j * 2, l * (N_GB // 2) + j + 1, n, 1)
                    steps.leave(N_GB // 2 - 1)
                n = dve.snap(l * NP + AT_OUT)

                def merged_low(g):
                    dve.wait_ge(m_hi, l * 4 + (g + 1))
                    v.tensor_tensor(Hs[:, 4 * g:4 * g + 4, S:2 * S], M[:, 4 * g:4 * g + 4, :],
                                    Hs[:, 4 * g:4 * g + 4, 0:S].bitcast(F32), ALU.subtract
                                    ).then_inc(m_lo, 1)

                for c in range(1, QC):
                    split_lo(n - 1, c)
                dve.wait_ge(m_sum, l * (N_GB // 2) + N_GB // 2)
                pair_out(n - 2, 0, QB[:, 0:2, :])
                for g in range(3):
                    merged_low(g)
                    split_lo(n, g)
                pair_out(n - 2, 1, QB[:, 2:4, :])
                add_b(KT - 2, l * (N_GB // 2) + N_GB // 2, n - 2, 1)
                steps.mark(v.memset(ACC[:], 0.0))
                merged_low(3)
                steps.wait()
                split_lo(n, 3)

                def add_x(tile, n, k):
                    xt, q = X[:, ds(tile, 2), :], k % 2
                    dve.wait_ge(multiplied, n * QC + (k + 2) * QC)
                    v.tensor_tensor(xt, xt, ps[:, 2 * q:2 * q + 2, S:2 * S], ALU.add
                                    ).then_inc(low_out, 1)
                    dve.wait_ge(low_out, n + (k + 1))
                    v.tensor_tensor(xt, xt, ps[:, 2 * q:2 * q + 2, 0:S], ALU.add
                                    ).then_inc(pairs_out, 1)

                with dve.Fori(0, N_OUT // 2 - 1) as j:
                    n = dve.snap(l * NP + AT_OUT + j * 2)
                    for k in range(2):
                        split_next(n, k)
                        add_x(j * 4 + 2 * k, n, k)
                        add_squares(l, j * 2 + k, k)
                n = dve.snap(l * NP + NP - 2)
                split_next(n, 0)
                add_x(KT - 4, n, 0)
                add_squares(l, N_OUT - 2, 0)
                add_x(KT - 2, n, 1)
                steps.leave(L)

            for t in range(Y_SPLIT):
                v.tensor_scalar(HEAD[:, t, :], X[:, t, :],
                                PAR[:, L * PARS + t:L * PARS + t + 1], None, ALU.mult
                                ).then_inc(y_vector, 1)
            inverse_rms(L)
            dve.wait_ge(inv_made, L + 1)
            for i in range(2):
                dve.wait_ge(y_turned, 2 * i + 1)
                cols = slice(i * D // 2, (i + 1) * D // 2)
                v.tensor_scalar(XROWS[:, 0, cols], px[:].rearrange("p a b -> p (a b)")[:, cols],
                                R4[:, 0:1], None, ALU.mult).then_inc(y_rows[0], 1)

        @block.tensor
        def _(pe):
            mm = nc.tensor.matmul

            def multiply(n, k, act_in, made=None, base=0, size=KQ, late=None):
                q = k % 2
                for c in range(QC):
                    if c == QC - 1 and late is not None:
                        late()
                    pe.wait_ge(lo_made, n * QC + (k * QC + QC + c + 1))
                    if c == 0:
                        pe.wait_ge(pairs_out, n + (k + 1))
                    for kk in range(KQ):
                        kt = c * KQ + kk
                        if made is not None and kt % size == 0:
                            pe.wait_ge(made, base + (kt // size + 1))
                        for t in range(2):
                            bank, cols = ps[:, 2 * q + t, :], slice(t * P, t * P + P)
                            mm(bank, WH[:, c, kk, cols], act_in[:, kt, :], start=(kt == 0), stop=False)
                            i = mm(bank[:, S:2 * S], WL[:, c, kk, cols], act_in[:, kt, 0:S],
                                   start=False, stop=(kt == KT - 1))
                    i.then_inc(multiplied, 1)

            def multiply_turned(n, k):
                q = k % 2
                for c in range(QC):
                    pe.wait_ge(lo_made, n * QC + (k * QC + QC + c + 1))
                    if c == 0:
                        pe.wait_ge(pairs_out, n + (k + 1))
                    for kk in range(KQ):
                        kt = c * KQ + kk
                        for s in range(ST):
                            bank = ps[:, 2 * q + s, :].rearrange("p (a b) -> p a b", a=2)
                            mm(bank, Hs[:, kt, s * P:(s + 1) * P], W[:, c, :, kk, :],
                               start=(kt == 0), stop=False)
                            i = mm(bank[:, 1, :], Hs[:, kt, S + s * P:S + (s + 1) * P],
                                   W[:, c, 0, kk, :], start=False, stop=(kt == KT - 1))
                    i.then_inc(multiplied, 1)

            pe.sem_inc(multiplied, QC)
            pe.wait_ge(ident_made, 1)
            for half, bank in enumerate((ps, px)):
                pe.wait_ge(x_rows_in[half], 16)
                for t in range(KT // 2):
                    for s in range(ST):
                        at = (t % 2) * S + s * P
                        tile = half * (KT // 2) + t
                        i = nc.tensor.transpose(bank[:, t // 2, at:at + P],
                                                XROWS[:, s, tile * P:(tile + 1) * P], IDENT[:])
                i.then_inc(x_turned, 1)
            pe.wait_ge(rows_in, 16 * len(row_loads))
            pe.wait_ge(pairs_out, 2)
            for b in range(L * PBLK + 1):
                rows = P if b < L * PBLK else KT
                i = nc.tensor.transpose(ps[:, b // 4, (b % 4) * P:(b % 4) * P + rows],
                                        PROWS[0:rows, b, :], IDENT[0:rows, 0:rows])
            i.then_inc(rows_turned, 1)
            pe.wait_ge(ones_made, 1)
            pe.wait_ge(x_in, 1)

            def sum_channels(bank, tiles, done):
                for t, tile in enumerate(tiles):
                    i = mm(px[:, bank, 0:S], ONES[:], tile, start=(t == 0),
                           stop=(t == len(tiles) - 1))
                i.then_inc(done, 1)

            def column_sums(tiles, first=True, last=True):
                for s in range(ST):
                    for t, tile in enumerate(tiles):
                        i = mm(px[:, s, 0:1], tile[:, s * P:(s + 1) * P], ONES[:, 0:1],
                               start=(first and t == 0), stop=(last and t == len(tiles) - 1))
                return i

            def spread_columns(bank, at, columns, done):
                for s in range(columns.shape[1]):
                    i = mm(px[:, bank, at + s * P:at + (s + 1) * P],
                           columns[:, s:s + 1].to_broadcast([P, P]), IDENT[:], start=True, stop=True)
                i.then_inc(done, 1)

            with pe.Fori(0, L) as l:
                n0 = pe.snap(l * NP)
                pe.wait_ge(inv_made, l + 1)
                spread_columns(0, S, R4[:, 0:ST], inv_spread)
                pe.wait_ge(par_made, 1)
                multiply(n0, 0, Hs, h_lo, l * (KT // 2), 2)

                pe.wait_ge(gw_lo, l + 1)
                for k in range(KT):
                    mm(px[:, 0, :], GS[:, k, 0:P], Hs[:, k, :], start=(k == 0), stop=False)
                    i = mm(px[:, 0, S:2 * S], GS[:, k, P:2 * P], Hs[:, k, 0:S],
                           start=False, stop=(k == KT - 1))
                i.then_inc(gates_mm, 1)

                def turn_gates():
                    pe.wait_ge(gates_made, l + 1)
                    for s in range(ST):
                        i = mm(px[:, s, 0:NG], GATES[:, s * P:(s + 1) * P], IDENT[0:NG, 0:NG],
                               start=True, stop=True)
                    i.then_inc(gates_turned, 1)

                multiply(n0, 1, Hs, late=turn_gates)
                pe.wait_ge(gcols_made, l + 1)
                for kind in range(2):
                    for s in range(ST):
                        dst = px[0:2 * H, 2, kind * S + s * P:kind * S + (s + 1) * P]
                        mm(dst, GC[:, s, 2 * kind, :], IDENT[:], start=True, stop=False)
                        i = mm(dst, GC[:, ST - 1 - s, 2 * kind + 1, :], IDENT[:, ::-1],
                               start=False, stop=True)
                i.then_inc(grows_mm, 1)
                multiply(n0, 2, Hs)
                multiply(n0, 3, Hs)
                pe.wait_ge(rows_made, l + 1)
                for s in range(ST):
                    for b, rows in enumerate((C_R, CB_R, N_R, ROWS[:, 1, :])):
                        at = (b // 2) * 4 * ST * H + s * 4 * H + (b % 2) * 2 * H
                        i = mm(px[:, 3, at:at + 2 * H], rows[:, s * P:(s + 1) * P],
                               IDENT[0:2 * H, 0:2 * H], start=True, stop=True)
                i.then_inc(ccol_mm, 1)
                with pe.Fori(2, N_GLU // 2) as j:
                    n = pe.snap(l * NP + j * 2)
                    multiply(n, 0, Hs)
                    multiply(n, 1, Hs)

                with pe.Fori(0, H) as h:
                    n = pe.snap(l * NP + AT_HEAD + h * 10)
                    u = pe.snap(l * H + h)

                    def spread_rms():
                        pe.wait_ge(ht_inv, u + 1)
                        spread_columns(0, S, R4[:, 0:ST], ht_spread)

                    multiply(n, 0, Hs)
                    pe.wait_ge(rs_made, u + 1)
                    for d in range(2):
                        i = mm(px[:, 1, d * S:(d + 1) * S], ONES[0:2 * H, :], RS[:, d, :],
                               start=True, stop=True)
                    i.then_inc(m_spread, 1)
                    for k in range(1, 4):
                        multiply(n, k, Hs)
                    multiply_turned(n, 4)
                    pe.wait_ge(qk_silu, u * 4 + 4)
                    for s in range(ST):
                        for k in range(HT):
                            i = mm(px[:, 0, s * S:(s + 1) * S], K_[:, k, s * P:(s + 1) * P],
                                   QB[:, k, :], start=(k == 0), stop=(k == HT - 1))
                    i.then_inc(scores, 1)
                    multiply_turned(n, 5)
                    pe.wait_ge(pw_summed, u + 1)
                    for d in range(2):
                        for lt in range(ST):
                            i = mm(px[:, 1, d * ST + lt:d * ST + lt + 1],
                                   EW[:, d, lt * P:(lt + 1) * P], ONES[:, 0:1],
                                   start=True, stop=True)
                    i.then_inc(dens, 1)
                    multiply(n, 6, Hs)
                    pe.wait_ge(dens_inv, u + 1)
                    spread_columns(0, 0, R4, dens_spread)
                    multiply(n, 7, Hs)
                    pe.wait_ge(a_made, u + 1)
                    pe.wait_ge(v_made, u + 2)
                    for k in range(HT):
                        for s in range(ST):
                            i = mm(px[:, 2 + k // 2, (k % 2) * S:(k % 2 + 1) * S],
                                   VS[:, s, k * P:(k + 1) * P], QB[:, s, :],
                                   start=(s == 0), stop=(s == ST - 1))
                    i.then_inc(ht_mm, 1)
                    multiply(n, 8, Hs)
                    pe.wait_ge(ht_added, u + 1)
                    column_sums([EW[:, 0, :]]).then_inc(ht_summed, 1)
                    multiply(n, 9, Hs, late=spread_rms)

                with pe.Fori(0, N_GA // 2) as j:
                    n = pe.snap(l * NP + AT_GA + j * 2)
                    multiply(n, 0, Hs)
                    multiply(n, 1, YC, ya_lo, l * H)

                n = pe.snap(l * NP + AT_ZB)
                multiply(n, 0, Hs)
                pe.wait_ge(conv_made, l + 1)
                sum_channels(0, [EW[:, t, :] for t in range(2)], mean_mm)
                multiply(n, 1, Hs)
                multiply(n, 2, Hs)
                pe.wait_ge(c_added, l * 4 + 4)
                sum_channels(1, [EW[:, t, :] for t in range(2)], c_summed)
                multiply(n, 3, Hs)
                with pe.Fori(2, N_ZB // 2) as j:
                    n = pe.snap(l * NP + AT_ZB + j * 2)
                    multiply(n, 0, Hs)
                    multiply(n, 1, Hs)

                with pe.Fori(0, N_GB // 2) as j:
                    n = pe.snap(l * NP + AT_GB + j * 2)
                    multiply(n, 0, Hs)
                    multiply(n, 1, YC, cb_lo, l * 4 + 1)
                with pe.Fori(0, N_OUT // 2) as j:
                    n = pe.snap(l * NP + AT_OUT + j * 2)
                    multiply(n, 0, Hs, m_lo, l * 4)
                    multiply(n, 1, Hs)
                pe.wait_ge(sq_added, l * (N_OUT - 1) + (N_OUT + 1))
                column_sums([ACC[:, t, :] for t in range(2)], last=False)
                pe.wait_ge(squared, l * N_OUT + N_OUT)
                column_sums([EW[:, t, :] for t in range(2, 4)], first=False).then_inc(summed, 1)

            pe.wait_ge(rms_made, L + 1)
            for half in range(2):
                for s, bank in enumerate((px, ps)):
                    for t in range(half * KT // 2, (half + 1) * KT // 2):
                        if s == 0:
                            pe.wait_ge(*((y_vector, t + 1) if t < Y_SPLIT else
                                         (y_scalar, t - Y_SPLIT + 1)))
                        i = nc.tensor.transpose(bank[:, t // 4, (t % 4) * P:(t % 4 + 1) * P],
                                                HEAD[:, t, s * P:(s + 1) * P], IDENT[:])
                    i.then_inc(y_turned, 1)


_INS = ["x", "norm_w", "w_in", "b_in", "qk_conv_w", "mlstm_norm_w", "w_a", "dw_w", "dw_b",
        "ln_w", "ln_b", "w_b", "w_out", "final_norm_w"]
_OUT = ((1, S, D), "float32")


def kernel(**inputs):
    import numpy as _np
    import concourse.bacc as _bacc
    from concourse import mybir as _mybir
    from concourse.bass_utils import run_bass_kernel_spmd as _run

    nc = _bacc.Bacc("TRN2", target_bir_lowering=False, num_devices=1)
    arrays, args = {}, []
    for name in _INS:
        a = _np.ascontiguousarray(inputs[name])
        arrays[f"in_{name}_dram"] = a
        args.append(nc.dram_tensor(f"in_{name}_dram", a.shape, _mybir.dt.from_np(a.dtype),
                                   kind="ExternalInput").ap())
    dt = _mybir.dt.from_np(_np.dtype(_OUT[1]))
    args.append(nc.dram_tensor("out_0_dram", _OUT[0], dt, kind="ExternalOutput").ap())
    build_trunk(nc, *args)
    r = _run(nc, [arrays], core_ids=[0])
    return r.results[0]["out_0_dram"]
```
